# Optimizing a Trainium2 kernel written in Bass

```python
import functools
import jax, jax.numpy as jnp
from jax import lax
import numpy as np

D_MODEL = 2048
BATCH = 1
SEQ = 512
DEPTH = 1
DEC_BATCH = 8
DEC_SEQ = 4
PAST_LEN = 2048
PAGE_SIZE = 128

N_HEADS = 8
HEAD_DIM = 128
ATTN_WIDTH = N_HEADS * HEAD_DIM
N_KV_HEADS = 2
GROUP = N_HEADS // N_KV_HEADS
KV_WIDTH = N_KV_HEADS * HEAD_DIM
IDX_HEADS = 16
IDX_DIM = 64
TOPK_MAX = 256
QBLOCK = 128
ROPE_THETA = 10000.0
CONV_WIDTH = D_MODEL - ATTN_WIDTH
CONV_KERNEL = 31
D_FF = -(-8 * D_MODEL // (3 * 256)) * 256
EPS = 1e-6
SPLIT_SIZES = (ATTN_WIDTH, KV_WIDTH, KV_WIDTH, IDX_HEADS * IDX_DIM, IDX_DIM, IDX_HEADS, 2 * CONV_WIDTH)
IN_WIDTH = sum(SPLIT_SIZES)

kernel_name = 'dsa_conformer_hybrid_step'

def rms_norm(x, g):
    xf = x.astype(jnp.float32)
    y = xf * lax.rsqrt(jnp.mean(xf * xf, axis=-1, keepdims=True) + EPS)
    return (y * g.astype(jnp.float32)).astype(x.dtype)

def layer_norm(x, g, b):
    xf = x.astype(jnp.float32)
    mu = jnp.mean(xf, axis=-1, keepdims=True)
    xc = xf - mu
    y = xc * lax.rsqrt(jnp.mean(xc * xc, axis=-1, keepdims=True) + EPS)
    return (y * g.astype(jnp.float32) + b.astype(jnp.float32)).astype(x.dtype)

def rope(x, pos):
    half = x.shape[-1] // 2
    freqs = ROPE_THETA ** (-jnp.arange(half, dtype=jnp.float32) / half)
    ang = pos.astype(jnp.float32)[:, None] * freqs[None, :]
    cos = jnp.cos(ang)[:, None, :]
    sin = jnp.sin(ang)[:, None, :]
    xf = x.astype(jnp.float32)
    x1, x2 = xf[..., :half], xf[..., half:]
    return jnp.concatenate([x1 * cos - x2 * sin, x2 * cos + x1 * sin], axis=-1).astype(x.dtype)

def project(n, w_in, pos):
    B, T, _ = n.shape
    p = n @ w_in
    splits = np.cumsum(SPLIT_SIZES)[:-1].tolist()
    q, k, v, qi, ki, wi, u = jnp.split(p, splits, axis=-1)
    q = rope(q.reshape(B, T, N_HEADS, HEAD_DIM), pos)
    k = rope(k.reshape(B, T, N_KV_HEADS, HEAD_DIM), pos)
    v = v.reshape(B, T, N_KV_HEADS, HEAD_DIM)
    qi = rope(qi.reshape(B, T, IDX_HEADS, IDX_DIM), pos)
    ki = rope(ki.reshape(B, T, 1, IDX_DIM), pos)[:, :, 0]
    wi = wi * (IDX_HEADS ** -0.5)
    return q, k, v, qi, ki, wi, u

def indexer_scores(qi, wi, ki):
    dots = jnp.einsum('bqhd,bsd->bqhs', qi, ki, preferred_element_type=jnp.float32) * (IDX_DIM ** -0.5)
    return jnp.einsum('bqh,bqhs->bqs', wi.astype(jnp.float32), jax.nn.relu(dots))

def sparse_attend(q, k_sel, v_sel, valid):
    B, Q = q.shape[:2]
    qg = q.reshape(B, Q, N_KV_HEADS, GROUP, HEAD_DIM)
    s = jnp.einsum('bqkgd,bqskd->bqkgs', qg, k_sel, preferred_element_type=jnp.float32) * (HEAD_DIM ** -0.5)
    s = jnp.where(valid[:, :, None, None, :], s, -jnp.inf)
    p = jax.nn.softmax(s, axis=-1).astype(v_sel.dtype)
    o = jnp.einsum('bqkgs,bqskd->bqkgd', p, v_sel)
    return o.reshape(B, Q, ATTN_WIDTH)

_gather_rows = jax.vmap(lambda rows, idx: rows[idx])

def prompt_attention(q, k, v, qi, ki, wi):
    B, T = q.shape[:2]
    topk = min(TOPK_MAX, T // 4)
    key_pos = jnp.arange(T)

    def block(i):
        start = i * QBLOCK
        qb = lax.dynamic_slice_in_dim(q, start, QBLOCK, axis=1)
        qib = lax.dynamic_slice_in_dim(qi, start, QBLOCK, axis=1)
        wib = lax.dynamic_slice_in_dim(wi, start, QBLOCK, axis=1)
        qpos = start + jnp.arange(QBLOCK)
        sc = indexer_scores(qib, wib, ki)
        sc = jnp.where((key_pos[None, :] <= qpos[:, None])[None], sc, -jnp.inf)
        _, idx = lax.top_k(sc, topk)
        valid = idx <= qpos[None, :, None]
        return sparse_attend(qb, _gather_rows(k, idx), _gather_rows(v, idx), valid)

    out = lax.map(block, jnp.arange(T // QBLOCK))
    return out.transpose(1, 0, 2, 3).reshape(B, T, ATTN_WIDTH)

def sample_attention(q, k_new, v_new, qi, ki_new, wi, cache_k, cache_v, cache_idx_k, page_table):
    B, T = q.shape[:2]
    past = page_table.shape[1] * PAGE_SIZE
    L = past + T
    topk = min(TOPK_MAX, L // 4)
    ki_past = cache_idx_k[page_table].reshape(B, past, IDX_DIM)
    ki_all = jnp.concatenate([ki_past, ki_new.astype(ki_past.dtype)], axis=1)
    qpos = past + jnp.arange(T)
    sc = indexer_scores(qi, wi, ki_all)
    sc = jnp.where((jnp.arange(L)[None, :] <= qpos[:, None])[None], sc, -jnp.inf)
    _, idx = lax.top_k(sc, topk)
    valid = idx <= qpos[None, :, None]
    in_past = idx < past
    pidx = jnp.minimum(idx, past - 1)
    phys = page_table[jnp.arange(B)[:, None, None], pidx // PAGE_SIZE]
    slot = pidx % PAGE_SIZE
    nidx = jnp.clip(idx - past, 0, T - 1)
    k_sel = jnp.where(in_past[..., None, None], cache_k[phys, slot], _gather_rows(k_new, nidx))
    v_sel = jnp.where(in_past[..., None, None], cache_v[phys, slot], _gather_rows(v_new, nidx))
    return sparse_attend(q, k_sel, v_sel, valid)

def conformer_conv(u, conv_prev, conv_dw, conv_dw_bias, conv_ln_g, conv_ln_b):
    a, gate = jnp.split(u, 2, axis=-1)
    g = a * jax.nn.sigmoid(gate)
    buf = jnp.concatenate([conv_prev.astype(g.dtype), g], axis=1)
    y = lax.conv_general_dilated(buf, conv_dw[:, None, :].astype(buf.dtype), window_strides=(1,),
                                 padding='VALID', dimension_numbers=('NWC', 'WIO', 'NWC'),
                                 feature_group_count=CONV_WIDTH)
    y = jax.nn.silu(layer_norm(y + conv_dw_bias, conv_ln_g, conv_ln_b))
    return y, buf[:, -(CONV_KERNEL - 1):]

def hybrid_layer(x, pos, conv_prev, attend, norm_attn, w_in, conv_dw, conv_dw_bias, conv_ln_g, conv_ln_b,
                 w_out, norm_ffn, w_gate, w_up, w_down):
    n = rms_norm(x, norm_attn)
    q, k, v, qi, ki, wi, u = project(n, w_in, pos)
    a = attend(q, k, v, qi, ki, wi)
    c, conv_new = conformer_conv(u, conv_prev, conv_dw, conv_dw_bias, conv_ln_g, conv_ln_b)
    h = x + jnp.concatenate([a, c], axis=-1) @ w_out
    n2 = rms_norm(h, norm_ffn)
    h = h + (jax.nn.silu(n2 @ w_gate) * (n2 @ w_up)) @ w_down
    return h, k, v, ki, conv_new

def setup_inputs(seed: int = 0) -> dict:
    key = jax.random.key(seed)
    ks = jax.random.split(key, 20)
    f32 = jnp.float32
    n_pages = PAST_LEN // PAGE_SIZE
    n_pool = (DEC_BATCH * n_pages * 5) // 4

    def nrm(k, shape, s):
        return jax.random.normal(k, shape, f32) * s

    page_table = jax.random.permutation(ks[6], n_pool)[:DEC_BATCH * n_pages].reshape(DEC_BATCH, n_pages).astype(jnp.int32)
    return {
        'x_prompt': nrm(ks[0], (BATCH, SEQ, D_MODEL), 1.0),
        'x_sample': nrm(ks[1], (DEC_BATCH, DEC_SEQ, D_MODEL), 1.0),
        'cache_k': nrm(ks[2], (DEPTH, n_pool, PAGE_SIZE, N_KV_HEADS, HEAD_DIM), 1.0),
        'cache_v': nrm(ks[3], (DEPTH, n_pool, PAGE_SIZE, N_KV_HEADS, HEAD_DIM), 1.0),
        'cache_idx_k': nrm(ks[4], (DEPTH, n_pool, PAGE_SIZE, IDX_DIM), 1.0),
        'state_conv': nrm(ks[5], (DEPTH, DEC_BATCH, CONV_KERNEL - 1, CONV_WIDTH), 0.5),
        'page_table': page_table,
        'norm_attn': 1.0 + nrm(ks[7], (DEPTH, D_MODEL), 0.05),
        'w_in': nrm(ks[8], (DEPTH, D_MODEL, IN_WIDTH), D_MODEL ** -0.5),
        'conv_dw': nrm(ks[9], (DEPTH, CONV_KERNEL, CONV_WIDTH), CONV_KERNEL ** -0.5),
        'conv_dw_bias': nrm(ks[10], (DEPTH, CONV_WIDTH), 0.02),
        'conv_ln_g': 1.0 + nrm(ks[11], (DEPTH, CONV_WIDTH), 0.05),
        'conv_ln_b': nrm(ks[12], (DEPTH, CONV_WIDTH), 0.02),
        'w_out': nrm(ks[13], (DEPTH, D_MODEL, D_MODEL), D_MODEL ** -0.5),
        'norm_ffn': 1.0 + nrm(ks[14], (DEPTH, D_MODEL), 0.05),
        'w_gate': nrm(ks[15], (DEPTH, D_MODEL, D_FF), D_MODEL ** -0.5),
        'w_up': nrm(ks[16], (DEPTH, D_MODEL, D_FF), D_MODEL ** -0.5),
        'w_down': nrm(ks[17], (DEPTH, D_FF, D_MODEL), D_FF ** -0.5),
        'norm_final': 1.0 + nrm(ks[18], (D_MODEL,), 0.05),
    }

def reference(x_prompt, x_sample, cache_k, cache_v, cache_idx_k, state_conv, page_table,
              norm_attn, w_in, conv_dw, conv_dw_bias, conv_ln_g, conv_ln_b, w_out, norm_ffn,
              w_gate, w_up, w_down, norm_final):
    B, T = x_prompt.shape[:2]
    Bs, Ts = x_sample.shape[:2]
    past = page_table.shape[1] * PAGE_SIZE
    pos_p = jnp.arange(T, dtype=jnp.int32)
    pos_s = past + jnp.arange(Ts, dtype=jnp.int32)
    conv_zero = jnp.zeros((B, CONV_KERNEL - 1, CONV_WIDTH), x_prompt.dtype)
    hp, hs = x_prompt, x_sample
    kp, vp, ip, cp, kss, vss, iss, css = [], [], [], [], [], [], [], []
    for l in range(DEPTH):
        weights = (norm_attn[l], w_in[l], conv_dw[l], conv_dw_bias[l], conv_ln_g[l], conv_ln_b[l],
                   w_out[l], norm_ffn[l], w_gate[l], w_up[l], w_down[l])
        hp, k_, v_, i_, c_ = hybrid_layer(hp, pos_p, conv_zero, prompt_attention, *weights)
        kp.append(k_); vp.append(v_); ip.append(i_); cp.append(c_)
        attend_s = functools.partial(sample_attention, cache_k=cache_k[l], cache_v=cache_v[l],
                                     cache_idx_k=cache_idx_k[l], page_table=page_table)
        hs, k_, v_, i_, c_ = hybrid_layer(hs, pos_s, state_conv[l], attend_s, *weights)
        kss.append(k_); vss.append(v_); iss.append(i_); css.append(c_)
    y_prompt = rms_norm(hp, norm_final)
    y_sample = rms_norm(hs, norm_final)
    return (y_prompt, y_sample,
            jnp.stack(kp), jnp.stack(vp), jnp.stack(ip), jnp.stack(cp),
            jnp.stack(kss), jnp.stack(vss), jnp.stack(iss), jnp.stack(css))


_drawn_inputs = setup_inputs


def setup_inputs(seed=0):
    import zlib

    import numpy as np

    out = dict(_drawn_inputs(seed))
    spreads = {}
    factors = {'conv_dw_bias': 3.185, 'conv_ln_b': 6.484}
    for name, (base, spread) in spreads.items():
        noise = np.random.default_rng([zlib.crc32(name.encode()), seed]).standard_normal(out[name].shape)
        drawn = base * np.exp(spread * noise) if base else spread * noise
        out[name] = __import__('jax').numpy.asarray(drawn.astype(out[name].dtype))
    for name, factor in factors.items():
        out[name] = (out[name] * factor).astype(out[name].dtype)
    return out
```

```python
from contextlib import ExitStack, contextmanager

import numpy as np
import concourse.bass as bass
from concourse import mybir

F32 = mybir.dt.float32
F32R = mybir.dt.float32r
BF16 = mybir.dt.bfloat16
I32 = mybir.dt.int32
ALU = mybir.AluOpType
ACT = mybir.ActivationFunctionType
AX = mybir.AxisListType

P = 128
D = 2048
SEQ = 512
B, T = 8, 4
NS = B * T
NT = SEQ + NS
HALF = NT // 2
KT = D // P
NH, NKV, HD = 8, 2, 128
GRP = NH // NKV
IH, ID = 16, 64
PAST, PAGE = 2048, 128
NPG = PAST // PAGE
CW_, CK = 1024, 31
CT = CW_ // P
DFF = 5632
EPS = 1e-6
KP_, KS_ = min(256, SEQ // 4), min(256, (PAST + T) // 4)
INVALID, TAKEN, MASKED = -3.0e38, -3.3e38, -1.0e30
ISCALE = float(ID) ** -0.5 * float(IH) ** -0.5
ASCALE = float(HD) ** -0.5

COL_Q, COL_K, COL_V, COL_QI, COL_KI = 0, 1024, 1280, 1536, 2560
COL_U = COL_KI + ID + IH
KIW = ID + IH

RING = 4
IB = 4
SLOTS = 4
SPP = 2
UK = 8
CH, CJ = 4, 11
DK = (6, 5)
P_QI = 0
P_U = P_QI + 4
P_Q = P_U + 8
P_K = P_Q + 4
P_V = P_K + 1
P_OUT = P_V + 1
P_FFN = P_OUT + KT // 2
P_CH = CJ + KT // 2
P_ALL = P_FFN + CH * P_CH
M_U, M_OUT, M_ALL = 2 * P_U + 1, 2 * P_OUT + 1, 2 * P_ALL + 1
NCONST = 13

NSK = PAST + NS
SW = [P * (i + 1) for i in range(4)]
SO = [0, 0, 256, 640]
BO = [0, 128, 384, 768]


class Unit:

    def __init__(self, p, q):
        self.n = 4 * p + 2 + q
        self.slot = (2 + q) % RING
        self.fill = p + (2 + q) // RING + 1
        self.first = isinstance(p, int) and self.n < RING


class Chain:

    def __init__(self, eng, sem):
        self.eng, self.sem, self.n, self.reg = eng, sem, 0, 0

    def link(self, ins):
        ins.then_inc(self.sem, 1)
        self.n += 1
        self.eng.wait_ge(self.sem, self.n + self.reg)

    @contextmanager
    def loop(self, start, end, per):
        n0 = self.n
        with self.eng.Fori(start, end) as i:
            self.reg = per * (i - start)
            yield i
        assert self.n == n0 + per
        self.n, self.reg = n0 + per * (end - start), 0


def build(nc, a, o):
    with ExitStack() as ctx:
        def sem(name):
            return ctx.enter_context(nc.semaphore(name))

        base = -(-nc.sbuf_base // 32) * 32
        ctx.enter_context(nc.sbuf_tensor("fence", [P, 53194], F32))

        def at(name, shape, dt, offset):
            return nc.alloc_sbuf_tensor_at(name, shape, dt, offset=base + offset)

        raw = at("raw", [P, RING, UK, P], F32, 0)
        whi = at("whi", [P, RING, UK, P], F32R, 16384)
        wlo = at("wlo", [P, RING, UK, P], F32R, 32768)
        xhi = at("xhi", [P, KT, NT], F32R, 49152)
        xlo = at("xlo", [P, KT, NT], F32R, 83968)
        C0 = 118784
        ident = at("ident", [P, P], F32, C0)
        ones = at("ones", [P, P], F32, C0 + 512)
        identb = at("identb", [P, P], BF16, C0 + 1024)
        vec = at("vec", [P, 56], F32, C0 + 1280)
        cw = at("cw", [P, CT, CK], F32, C0 + 1504)
        stat = at("stat", [P, 64], F32, C0 + 2496)
        S0 = C0 + 2816
        qT = at("qT", [P, 8, NT], F32, S0)
        kT = at("kT", [P, NKV, NT], F32, S0 + 17408)
        vN = at("vN", [P, 5, 256], F32, S0 + 21760)
        biasS = at("biasS", [NS, NSK], BF16, S0 + 26880)
        biasP = at("biasP", [P, 1280], BF16, S0 + 31040)
        qpad = at("qpad", [P, B, NKV, 32], F32, S0 + 33600)
        wiP = at("wiP", [P, 4, IH], F32, S0 + 35648)
        rowsel = at("rowsel", [NS, 2, P], BF16, S0 + 35904)
        tab = at("tab", [P, 4, NT], F32, S0 + 36672)
        rstd1 = at("rstd1", [P, NT], F32, S0 + 45376)
        kiT = at("kiT", [P, NT], F32, S0 + 47552)
        scP = at("scP", [P, 1152], F32, S0 + 49728)
        scS = at("scS", [NS, NSK], F32, S0 + 54336)
        R0 = S0 + 62656
        xN = at("xN", [P, 2, D], F32, R0)
        xg = at("xg", [P, 2, 4, P], F32, R0 + 16384)
        rowselF = at("rowselF", [NS, 2, P], F32, R0 + 20480)
        causF = at("causF", [P, P], F32, R0 + 21504)
        xT = at("xT", [P, 2, KT, P], F32, S0)
        junk = at("junk", [P, D], F32, S0 + 17408)
        vecN = at("vecN", [56, P], F32, S0 + 25600)
        cwN = at("cwN", [CK, CW_], F32, S0 + 26112)
        diag = at("diag", [P, 5, P], F32, S0 + 49728)
        idxN = at("idxN", [P, IB, NPG, ID], F32, R0)
        idxT = at("idxT", [P, 2, NPG // 2, P], F32, R0 + 16384)
        kiN = at("kiN", [P, 5, ID], F32, R0 + 24576)
        rel = at("rel", [P, 2, 512], F32, S0 + 17408)
        wT = at("wT", [IH, NT], F32, S0 + 21760)
        qiS = at("qiS", [P, B, 2, IH, T], F32, S0 + 23936)
        wsel = at("wsel", [P, B, 2, NS], F32, S0 + 28032)
        hsel = at("hsel", [IH, P], F32, S0 + 30080)
        tsel = at("tsel", [P, NS], F32, S0 + 30592)
        tailm = at("tailm", [NS, NS], F32, S0 + 30720)
        rt = at("rt", [P, NT], F32, R0 + 23936)
        gbuf = at("gbuf", [P, SEQ + CK - 1 + B * (CK - 1 + T)], F32, R0)
        y = at("y", [P, CT, NT], F32, R0 + 3264)
        ga = at("ga", [P, NT], F32, R0 + 20672)
        sg = at("sg", [P, NT], F32, R0 + 22848)
        tg = at("tg", [P, P], F32, R0 + 26112)
        stN = at("stN", [120, 2, CW_], F32, S0)
        stT = at("stT", [P, CT, B * (CK - 1)], F32, S0 + 8192)
        cout = at("cout", [CK - 1 + NS, CW_], F32, S0 + 26880)
        vT = at("vT", [P, NKV, NT], F32, S0 + 49728)
        kN = at("kN", [P, 5, 256], F32, S0 + 38848)
        mu = at("mu", [P, NT], F32, S0 + 45376)
        rl = at("rl", [P, NT], F32, S0 + 36672)
        sq = at("sq", [P, 2, NT], F32, R0 + 20672)
        pP = at("pP", [P, 3, SEQ], F32, S0 + 36672)
        pPT = at("pPT", [P, 2, 4, P], F32, S0 + 42816)
        pages = at("pages", [P, SLOTS, 4, 256], F32, R0)
        kpT = at("kpT", [P, 2, NKV, 512], F32, R0 + 16384)
        pS = at("pS", [P, NSK], F32, S0 + 36672)
        pST = at("pST", [P, 17, P], F32, S0 + 44992)
        h = at("h", [P, KT, NT], F32, S0)
        hidh = at("hidh", [P, CJ, NT], F32R, S0 + 34816)
        hidl = at("hidl", [P, CJ, NT], F32R, S0 + 58752)
        gt = at("gt", [P, NT], F32, S0 + 82688)
        ut = at("ut", [P, NT], F32, S0 + 84864)
        rstd2 = at("rstd2", [P, NT], F32, S0 + 87040)
        hg = at("hg", [P, KT, NT], F32, S0 + 34816)
        xTr = at("xTr", [P, 2, NT], F32, S0 + 69632)
        sq2 = at("sq2", [P, NT], F32, S0 + 73984)
        sqa = at("sqa", [P, NT], F32, S0 + 76160)
        gfb = at("gfb", [P, D], F32, S0 + 34816)
        yo = at("yo", [P, 2, D], F32, S0 + 43008)
        junk2 = at("junk2", [P, D], F32, S0 + 59392)

        page = at("page", [P, B * NPG], I32, S0 + 35904)[64:65, :]
        m8 = at("m8", [P, 4, 8], F32, S0 + 36416)
        ps = ctx.enter_context(nc.psum_tensor("ps", [P, 8, 512], F32))

        s_raw = [sem(f"s_raw{i}") for i in range(RING)]
        s_hi, s_lo = sem("s_hi"), sem("s_lo")
        s_mm = sem("s_mm")
        s_ev = sem("s_ev")
        s_proj = sem("s_proj")
        s_const, s_cst = sem("s_const"), sem("s_cst")
        s_ct, s_cc = sem("s_ct"), sem("s_cc")
        s_xn = [sem("s_xn0"), sem("s_xn1")]
        s_xt, s_xe, s_xg, s_xh, s_xl = sem("s_xt"), sem("s_xe"), sem("s_xg"), sem("s_xh"), sem("s_xl")
        s_ssq = sem("s_ssq")
        s_sp = [sem("s_sp0"), sem("s_sp1")]
        s_rs, s_rd, s_rb, s_tab = sem("s_rs"), sem("s_rd"), sem("s_rb"), sem("s_tab")
        s_dve, s_pool = sem("s_dve"), sem("s_pool")
        s_wt, s_wtc = sem("s_wt"), sem("s_wtc")
        s_is, s_ir, s_ia = sem("s_is"), sem("s_ir"), sem("s_ia")
        s_caus = sem("s_caus")
        s_page = sem("s_page")
        s_ik = [sem(f"s_ik{i}") for i in range(IB)]
        s_iks = [sem(f"s_iks{i}") for i in range(IB)]
        s_it, s_ic = sem("s_it"), sem("s_ic")
        s_dt, s_dr, s_hs, s_xs = sem("s_dt"), sem("s_dr"), sem("s_hs"), sem("s_xs")
        s_st, s_stt, s_stc = sem("s_st"), sem("s_stt"), sem("s_stc")
        s_sg, s_conv, s_tg, s_tt, s_co = sem("s_sg"), sem("s_conv"), sem("s_tg"), sem("s_tt"), sem("s_co")
        s_topk = sem("s_topk")
        s_bias = sem("s_bias")
        s_nt, s_nc = sem("s_nt"), sem("s_nc")
        s_l1, s_yc, s_sqd, s_sqm, s_l2, s_sd, s_yn, s_yh = (sem("s_" + x) for x in
                                                           ("l1", "yc", "sqd", "sqm", "l2", "sd", "yn", "yh"))
        s_mix = sem("s_mix")
        s_qp = sem("s_qp")
        s_s, s_nm, s_p, s_pn, s_pt, s_pc, s_o, s_oh, s_ol = (sem("s_" + x) for x in
                                                             ("s", "nm", "p", "pn", "pt", "pc", "o", "oh", "ol"))
        s_pg = [sem(f"s_pg{i}") for i in range(SLOTS)]
        s_pgp = [sem(f"s_pgp{i}") for i in range(SLOTS)]
        s_chunk = sem("s_chunk")
        s_kca, s_kcd, s_ks = sem("s_kca"), sem("s_kcd"), sem("s_ks")
        s_gb, s_gm, s_gp, s_gn, s_gt, s_gc, s_gh, s_gl = (sem("s_g" + x) for x in "bmpntchl")
        s_xr = [sem("s_xr0"), sem("s_xr1")]
        s_h, s_sqh, s_sqs = sem("s_h"), sem("s_sqh"), sem("s_sqs")
        s_r2, s_r2s, s_r2d = sem("s_r2"), sem("s_r2s"), sem("s_r2d")
        s_n2h, s_n2 = sem("s_n2h"), sem("s_n2")
        s_silu, s_hm, s_hh, s_hid = sem("s_silu"), sem("s_hm"), sem("s_hh"), sem("s_hid")
        s_gf, s_yt, s_ys, s_yd = (sem("s_" + x) for x in ("gf", "yt", "ys", "yd"))
        s_nm2 = sem("s_nm2")
        s_yo = [sem("s_yo0"), sem("s_yo1")]
        s_kio, s_cvo, s_ko, s_vo = sem("s_kio"), sem("s_cvo"), sem("s_ko"), sem("s_vo")

        w_in = a["w_in"][0].rearrange("(t p) n -> p t n", p=P)
        w_out = a["w_out"][0].rearrange("(t p) n -> p t n", p=P)
        w_gate = a["w_gate"][0].rearrange("(t p) n -> p t n", p=P)
        w_up = a["w_up"][0].rearrange("(t p) n -> p t n", p=P)
        w_down = a["w_down"][0].rearrange("(t p) n -> p t n", p=P)
        x_rows = [a["x_prompt"][0][P * i:P * i + P, :] for i in range(4)] + [
            a["x_sample"].rearrange("b t d -> (b t) d")]
        tok = [P] * 4 + [NS]
        xT_dram = a["xT_dram"].rearrange("(t p) n -> p t n", p=P)
        kc = a["cache_k"][0].rearrange("n s k d -> n s (k d)")
        vc = a["cache_v"][0].rearrange("n s k d -> n s (k d)")
        ic = a["cache_idx_k"][0]
        NPOOL = ic.shape[0]

        block = ctx.enter_context(nc.Block())

        def halves(ap):
            return ap.rearrange("p (h n) -> p h n", h=2)

        def tile_of(buf, j):
            return buf[:, bass.ds(j, 1), :].rearrange("p a (h n) -> p (a h) n", h=2)

        def acc(slot, p0=0, p1=P):
            return ps[p0:p1, 2 * slot:2 * slot + 2, 0:HALF]

        flat = ps[:, :, :].rearrange("p b n -> p (b n)")
        score_row = flat[:, 0:NSK]

        def row_banks(i):
            return flat[0:tok[i], D * (i % 2):D * (i % 2) + D]

        def pv_bank(kv):
            return ps[:, (7, 4)[kv], 0:4 * GRP * T].rearrange("p (b g t) -> p g b t", b=4, g=GRP)

        def mixed(x, kv, g):
            c0 = SEQ + 4 * T * g
            return x[:, GRP * kv:GRP * kv + GRP, c0:c0 + 4 * T].rearrange("p g (b t) -> p g b t", b=4)

        def rows_out(eng, dst, src, last, width, sem_done):
            eng.copy(dst[:, 0:4, :], src.rearrange("p (i d) -> p i d", i=4))
            eng.copy(dst[0:NS, 4, :], last).then_inc(sem_done, 1)

        def store_rows(eng, prompt, sample, src, sem_done):
            eng.dma_start(prompt.rearrange("(i p) d -> p i d", p=P), src[:, 0:4, :]).then_inc(sem_done, 16)
            eng.dma_start(sample, src[0:NS, 4, :]).then_inc(sem_done, 16)

        def index_pages(eng, b, g0, g1, landed):
            if b >= IB:
                eng.wait_ge(s_it, 2 * (b - IB + 1))
            with eng.Fori(g0, g1) as g:
                pg = eng.value_load(page[0:1, bass.ds(b * NPG + g, 1)], min_val=0, max_val=NPOOL - 1)
                eng.dma_start(idxN[:, b % IB, bass.ds(g, 1), :].rearrange("p a d -> p (a d)"),
                              ic[bass.ds(pg, 1), :, :].rearrange("a s d -> (a s) d")).then_inc(landed[b % IB], 16)

        def page_chunks(eng, k0, k1, landed):
            def chunks(src, n, p0, first):
                for s in range(SLOTS):
                    if not first:
                        eng.wait_ge(s_chunk, n + s - SLOTS + 1)
                    for k in range(k0, k1):
                        pg = eng.value_load(page[0:1, bass.ds(p0 + 4 * s + k, 1)], min_val=0, max_val=NPOOL - 1)
                        eng.dma_start(pages[:, s, k, :], src[bass.ds(pg, 1), :, :].rearrange("a s d -> (a s) d")
                                      ).then_inc(landed[s], 16)

            eng.wait_ge(s_page, 16)
            eng.wait_ge(s_mix, CT)
            for g in range(2):
                for v, src in enumerate((kc, vc)):
                    first = g == 0 and v == 0
                    if first:
                        chunks(src, 0, 0, True)
                    with eng.Fori(1 if first else 0, 16 // SLOTS) as r:
                        chunks(src, 32 * g + 16 * v + SLOTS * r, 64 * g + 4 * SLOTS * r, False)

        @block.sync
        def _(sp):
            def load(u, src, k=UK, cols=P):
                if not u.first:
                    sp.wait_ge(s_lo, u.n - RING + 1)
                sp.dma_start(raw[:, u.slot, 0:k, 0:cols], src).then_inc(s_raw[u.slot], 16)

            def col(w, c, hf):
                return w[:, UK * hf:UK * hf + UK, bass.ds(c, P)]

            for i in range(5):
                if i >= 2:
                    sp.wait_ge(s_xt, 4 * (i - 1))
                    sp.wait_ge(s_ssq, i - 1)
                sp.dma_start(xN[0:tok[i], i % 2, :], x_rows[i]).then_inc(s_xn[i % 2], 16)
                if i == 1:
                    for hf in range(2):
                        load(Unit(-1, 2 + hf), w_in[:, UK * hf:UK * hf + UK, COL_KI:COL_KI + KIW], cols=KIW)
                    for hf in range(2):
                        load(Unit(0, hf), col(w_in, COL_QI, hf))
            for hf in range(2):
                load(Unit(0, 2 + hf), col(w_in, COL_QI + P, hf))
            with sp.Fori(1, 4) as i:
                for q in range(4):
                    load(Unit(P_QI + i, q), col(w_in, COL_QI + 256 * i + P * (q // 2), q % 2))
            def conv_input(i):
                for q in range(4):
                    load(Unit(P_U + i, q), col(w_in, COL_U + P * i + CW_ * (q // 2), q % 2))

            conv_input(0)
            sp.wait_ge(s_page, 16)
            for b in range(IB, B):
                index_pages(sp, b, NPG // 2, NPG, s_iks)
            with sp.Fori(1, 8) as i:
                conv_input(i)
            with sp.Fori(0, 4) as i:
                for q in range(4):
                    load(Unit(P_Q + i, q), col(w_in, COL_Q + 256 * i + P * (q // 2), q % 2))
            for q in range(8):
                load(Unit(P_K, q), col(w_in, COL_K + P * (q // 2), q % 2))
            def residual(i, s):
                sp.dma_start(xTr[:, s, :], xT_dram[:, bass.ds(2 * i + s, 1), :].rearrange("p a n -> p (a n)")
                             ).then_inc(s_xr[s], 16)

            for q in range(4):
                load(Unit(P_OUT, q), col(w_out, P * (q // 2), q % 2))
            page_chunks(sp, 0, SPP, s_pg)
            sp.wait_ge(s_sp[0], 48)
            sp.wait_ge(s_sp[1], 32)
            sp.wait_ge(s_gl, 4)
            for s in range(2):
                residual(0, s)
            with sp.Fori(1, 8) as i:
                for q in range(4):
                    load(Unit(P_OUT + i, q), col(w_out, 256 * i + P * (q // 2), q % 2))
                    if q % 2:
                        sp.wait_ge(s_ev, M_OUT + 2 * i + q // 2 - 1)
                        residual(i, q // 2)
            with sp.Fori(0, CH) as c:
                p0 = P_FFN + P_CH * c
                with sp.Fori(0, CJ) as j:
                    for q in range(4):
                        load(Unit(p0 + j, q), col((w_gate, w_up)[q // 2], P * CJ * c + P * j, q % 2))
                with sp.Fori(0, 8) as i:
                    for q in range(4):
                        hf = q % 2
                        load(Unit(p0 + CJ + i, q),
                             w_down[:, bass.ds(CJ * c + DK[0] * hf, DK[hf]), bass.ds(256 * i + P * (q // 2), P)],
                             k=DK[hf])
            sp.wait_ge(s_mm, 2 * M_ALL)
            sp.dma_start(gfb[:, :], a["norm_final"].partition_broadcast(P)).then_inc(s_gf, 16)
            for i in range(5):
                sp.wait_ge(s_yd, i + 1)
                dst = o["y_prompt"][0][P * i:P * i + P, :] if i < 4 else o["y_sample"].rearrange("b t d -> (b t) d")
                sp.dma_start(dst, yo[0:tok[i], i % 2, :]).then_inc(s_yo[i % 2], 16)
            sp.wait_ge(s_yo[0], 48)
            sp.wait_ge(s_yo[1], 32)
            sp.wait_ge(s_kio, 32)
            sp.wait_ge(s_cvo, 48)
            sp.wait_ge(s_ko, 32)
            sp.wait_ge(s_vo, 32)

        @block.gpsimd
        def _(pool):
            pool.dma_start(ident[:, :], a["c_ident"]).then_inc(s_const, 16)
            pool.dma_start(vecN[0:16, :], a["norm_attn"][0].rearrange("(k p) -> k p", p=P)).then_inc(s_const, 16)
            pool.dma_start(vecN[16:32, :], a["norm_ffn"][0].rearrange("(k p) -> k p", p=P)).then_inc(s_const, 16)
            for n, name in enumerate(("conv_dw_bias", "conv_ln_g", "conv_ln_b")):
                pool.dma_start(vecN[32 + 8 * n:40 + 8 * n, :], a[name][0].rearrange("(k p) -> k p", p=P)
                               ).then_inc(s_const, 16)
            pool.dma_start(cwN[:, :], a["conv_dw"][0]).then_inc(s_const, 16)
            pool.dma_start(page, a["page_table"].rearrange("(o b) n -> o (b n)", o=1)).then_inc(s_page, 16)
            pool.dma_start(tab[:, :, :], a["c_rope"]).then_inc(s_const, 16)
            pool.dma_start(rowselF[:, :, :], a["c_rowsel"]).then_inc(s_const, 16)
            pool.dma_start(causF[:, :], a["c_caus"]).then_inc(s_const, 16)
            nc.gpsimd.memset(ones[:, :], 1.0).then_inc(s_pool, 1)
            nc.gpsimd.memset(qpad[:, :, :, :], 0.0).then_inc(s_pool, 1)
            nc.gpsimd.memset(stat[:, :], EPS).then_inc(s_pool, 1)
            c0 = 0
            for i in range(5):
                pool.wait_ge(s_xe, 4 * (i + 1))
                pool.dma_start(xT_dram[:, :, c0:c0 + tok[i]], xT[:, i % 2, :, 0:tok[i]]).then_inc(s_sp[i % 2], 16)
                c0 += tok[i]
            pool.wait_ge(s_xl, 20)
            pool.wait_ge(s_ssq, 5)
            pool.wait_ge(s_caus, 1)
            for dst, name in ((hsel, "c_hsel"), (tsel, "c_tsel"), (tailm, "c_tail")):
                pool.dma_start(dst[:, :], a[name]).then_inc(s_const, 16)

            pool.wait_ge(s_page, 16)
            for b in range(B):
                index_pages(pool, b, 0, NPG if b < IB else NPG // 2, s_ik)
                if b == IB - 1:
                    pool.wait_ge(s_ia, 3 * IH)
                    for i in range(1, 4):
                        v = scP[:, SO[i] + SW[i] - P:SO[i] + SW[i]]
                        nc.gpsimd.affine_select(out=v, in_=v, compare_op=ALU.is_ge, fill=INVALID, base=0,
                                                pattern=[[-1, P]], channel_multiplier=1).then_inc(s_pool, 1)
            pool.wait_ge(s_nc, 1)
            store_rows(pool, o["idx_k_prompt"][0, 0], o["idx_k_sample"][0].rearrange("b t d -> (b t) d"), kiN, s_kio)
            pool.wait_ge(s_hs, 3 * B)
            pool.dma_start(stN[:, :, :], a["state_conv"][0].rearrange("(a b) s c -> (b s) a c", a=2)).then_inc(s_st, 16)
            pool.dma_start(o["conv_sample"][0][:, 0:CK - 1 - T, :], a["state_conv"][0][:, T:CK - 1, :]
                           ).then_inc(s_cvo, 16)
            pool.wait_ge(s_co, CT)
            pool.dma_start(o["conv_prompt"][0, 0], cout[0:CK - 1, :]).then_inc(s_cvo, 16)
            pool.dma_start(o["conv_sample"][0][:, CK - 1 - T:CK - 1, :], cout[CK - 1:CK - 1 + NS, :]
                           ).then_inc(s_cvo, 16)
            pool.wait_ge(s_nc, 2)
            store_rows(pool, o["k_prompt"][0, 0].rearrange("s k d -> s (k d)"),
                     o["k_sample"][0].rearrange("b t k d -> (b t) (k d)"), kN, s_ko)
            pool.wait_ge(s_nc, 3)
            store_rows(pool, o["v_prompt"][0, 0].rearrange("s k d -> s (k d)"),
                     o["v_sample"][0].rearrange("b t k d -> (b t) (k d)"), vN, s_vo)
            page_chunks(pool, SPP, 4, s_pgp)

        @block.scalar
        def _(act):
            def hi(u, cols=P):
                act.wait_ge(s_raw[u.slot], 16 * u.fill)
                if not u.first:
                    act.wait_ge(s_mm, u.n - RING + 1)
                nc.scalar.copy(whi[:, u.slot, :, 0:cols], raw[:, u.slot, :, 0:cols]).then_inc(s_hi, 1)

            def x_high(n):
                i, kb = divmod(n, 4)
                act.wait_ge(s_xg, n + 1)
                nc.scalar.copy(xhi[:, 4 * kb:4 * kb + 4, P * i:P * i + tok[i]], xg[:, n % 2, :, 0:tok[i]]
                               ).then_inc(s_xh, 1)

            act.wait_ge(s_ct, 1)
            nc.scalar.copy(vec[:, :], ps[:, 0, 0:56]).then_inc(s_cc, 1)
            nc.scalar.copy(cw[:, :, :], ps[:, 1, 0:CT * CK].rearrange("p (c k) -> p c k", c=CT)).then_inc(s_cc, 1)
            for i in range(5):
                if i >= 2:
                    act.wait_ge(s_sp[i % 2], 16 * (i // 2))
                for kb in range(4):
                    n = 4 * i + kb
                    act.wait_ge(s_xt, n + 1)
                    nc.scalar.copy(xT[:, i % 2, 4 * kb:4 * kb + 4, 0:tok[i]],
                                   ps[:, 4 + kb, :].rearrange("p (k n) -> p k n", k=4)[:, :, 0:tok[i]]
                                   ).then_inc(s_xe, 1)
                    if n >= 1:
                        x_high(n - 1)
                if i == 0:
                    act.wait_ge(s_pool, 3)
                    act.wait_ge(s_cc, 2)
                else:
                    act.wait_ge(s_ssq, i)
                nc.scalar.activation(junk[0:tok[i], :], xN[0:tok[i], i % 2, :], ACT.Square,
                                     accum_out=stat[0:tok[i], 8 + i:9 + i]).then_inc(s_ssq, 1)
            x_high(19)
            act.wait_ge(s_ssq, 5)
            nc.scalar.activation(stat[:, 16:21], stat[:, 8:13], ACT.Sqrt, bias=stat[:, 0:1], scale=1.0 / D
                                 ).then_inc(s_rs, 1)
            for q in range(6):
                hi(Unit(-1, 2 + q), KIW if q < 2 else P)

            def hi4(p):
                for q in range(4):
                    hi(Unit(p, 4 + q))

            with act.Fori(0, 4) as i:
                hi4(P_QI + i)

            n = 0
            for i in range(1, 4):
                for hh in range(IH):
                    act.wait_ge(s_is, n + 1)
                    if n >= 2:
                        act.wait_ge(s_ia, n - 1)
                    nc.scalar.activation(rel[:, n % 2, 0:SW[i]], ps[:, 4 + n % 4, 0:SW[i]], ACT.Relu).then_inc(s_ir, 1)
                    n += 1
            act.wait_ge(s_nt, 1)
            act.wait_ge(s_xl, 20)
            act.wait_ge(s_proj, 9)
            rows_out(nc.scalar, kiN, ps[:, 4, 0:4 * ID], ps[0:NS, 5, 0:ID], ID, s_nc)
            act.wait_ge(s_ia, 3 * IH)
            for b in range(B):
                for g in range(2):
                    act.wait_ge(s_it, 2 * b + g + 1)
                    if b >= 2:
                        act.wait_ge(s_dt, 3 * (b - 1))
                    nc.scalar.copy(idxT[:, b % 2, 4 * g:4 * g + 4, :], ps[:, 5, :].rearrange("p (k n) -> p k n", k=4)
                                   ).then_inc(s_ic, 1)
                for c in range(3):
                    n = 3 * b + c
                    r, w = (P, 512) if c < 2 else (P // 2, NS)
                    act.wait_ge(s_dt, n + 1)
                    if n >= 2:
                        act.wait_ge(s_hs, n - 1)
                    nc.scalar.activation(rel[0:r, n % 2, 0:w], ps[0:r, 6 + n % 2, 0:w], ACT.Relu).then_inc(s_dr, 1)
            for c in range(CT):
                act.wait_ge(s_stt, c + 1)
                nc.scalar.copy(stT[:, c, :], ps[:, 4 + c % 4, 0:240]).then_inc(s_stc, 1)

            def sigmoid_gate(m):
                act.wait_ge(s_ev, m + 1)
                nc.scalar.activation(sg[:, :], sg[:, :], ACT.Sigmoid).then_inc(s_sg, 1)

            def state_rows(c):
                act.wait_ge(s_tt, c + 1)
                nc.scalar.copy(cout[:, bass.ds(c * P, P)], ps[0:CK - 1 + NS, 6, 0:P]).then_inc(s_co, 1)

            hi4(P_U)
            sigmoid_gate(M_U + 1)
            with act.Fori(1, CT) as i:
                hi4(P_U + i)
                sigmoid_gate(M_U + 2 * i + 1)
                state_rows(i - 1)
            hi4(P_Q)
            state_rows(CT - 1)
            with act.Fori(1, 4) as i:
                hi4(P_Q + i)
            hi4(P_K)
            hi4(P_V)
            act.wait_ge(s_nt, 2)
            rows_out(nc.scalar, kN, flat[:, 2048:3072], ps[0:NS, 6, 0:256], 256, s_nc)
            act.wait_ge(s_nt, 3)
            rows_out(nc.scalar, vN, flat[:, 2048:3072], ps[0:NS, 6, 0:256], 256, s_nc)
            for c in range(CT):
                act.wait_ge(s_yc, c + 1)
                if c >= 2:
                    act.wait_ge(s_sqm, c - 1)
                nc.scalar.activation(sq[:, c % 2, :], y[:, c, :], ACT.Square).then_inc(s_sqd, 1)
            act.wait_ge(s_l2, 1)
            nc.scalar.activation(halves(rl[:, :]), ps[:, 4:6, 0:HALF], ACT.Sqrt, bias=stat[:, 0:1], scale=1.0 / CW_
                                 ).then_inc(s_sd, 1)
            for c in range(CT):
                act.wait_ge(s_yn, c + 1)
                nc.scalar.activation(y[:, c, :], y[:, c, :], ACT.Silu, bias=vec[:, 48 + c:49 + c],
                                     scale=vec[:, 40 + c:41 + c]).then_inc(s_yh, 1)
                act.wait_ge(s_yh, 2 * c + 1)
                nc.scalar.copy(xhi[:, 8 + c, :], y[:, c, :]).then_inc(s_yh, 1)

            act.wait_ge(s_ko, 32)
            for x in range(32 + 3):
                if x < 32:
                    w = SW[x // 8]
                    act.wait_ge(s_nm, x + 1)
                    if x >= 3:
                        act.wait_ge(s_pt, x - 2)
                    nc.scalar.activation(pP[:, x % 3, 0:w], ps[:, (4, 5, 0, 1)[x % 4], 0:w], ACT.Exp,
                                         bias=stat[:, 24 + x % 4:25 + x % 4], scale=ASCALE,
                                         accum_out=stat[:, 28 + x % 4:29 + x % 4]).then_inc(s_p, 1)
                if 0 <= x - 2 < 32:
                    z = x - 2
                    act.wait_ge(s_pt, z + 1)
                    if z >= 2:
                        act.wait_ge(s_o, z - 1)
                    nb = z // 8 + 1
                    nc.scalar.copy(pPT[:, z % 2, 0:nb, :], ps[:, (6, 2)[z % 2], 0:P * nb].rearrange(
                        "p (k n) -> p k n", k=nb)).then_inc(s_pc, 1)
                if x >= 3 and (x - 3) % 4 == 3:
                    z = x - 3
                    act.wait_ge(s_o, z + 1)
                    h0, q0 = z % 8 - 3, P * (z // 8)
                    nc.scalar.copy(xhi[:, h0:h0 + 4, q0:q0 + P], ps[:, (7, 3)[z // 4 % 2], :].rearrange(
                        "p (k n) -> p k n", k=4)).then_inc(s_oh, 1)

            for g in range(2):
                for q in range(16 * g, 16 * g + 16):
                    act.wait_ge(s_chunk, 16 * g + q + 1)
                    if q >= 2:
                        act.wait_ge(s_ks, q - 1)
                    nc.scalar.copy(kpT[:, q % 2, 0, :], ps[:, 5, :]).then_inc(s_kca, 1)
                act.wait_ge(s_gm, g + 1)
                if g == 0:
                    act.wait_ge(s_o, 32)
                else:
                    act.wait_ge(s_gt, 5)
                nc.scalar.activation(pS[:, :], score_row, ACT.Exp, bias=stat[:, 32:33], scale=ASCALE,
                                     accum_out=stat[:, 33:34]).then_inc(s_gp, 1)
                for c in range(5):
                    act.wait_ge(s_gt, 5 * g + c + 1)
                    if g == 1 and c == 0:
                        act.wait_ge(s_gl, 2)
                    if c < 4:
                        nc.scalar.copy(pST[:, 4 * c:4 * c + 4, :], ps[:, 5 + c % 2, :].rearrange(
                            "p (k n) -> p k n", k=4)).then_inc(s_gc, 1)
                    else:
                        nc.scalar.copy(pST[0:NS, 16, :], ps[0:NS, 5, 0:P]).then_inc(s_gc, 1)
                act.wait_ge(s_chunk, 32 * g + 32)
                for kv in range(NKV):
                    nc.scalar.copy(mixed(xhi, kv, g), pv_bank(kv)).then_inc(s_gh, 1)

            def square(j):
                act.wait_ge(s_h, j + 1)
                act.wait_ge(s_sqs, j + 1)
                nc.scalar.activation(halves(sq2[:, :]), tile_of(h, j), ACT.Square).then_inc(s_sqh, 1)

            with act.Fori(0, 8) as i:
                for s in range(2):
                    hi(Unit(P_OUT + i, 4 + 2 * s))
                    hi(Unit(P_OUT + i, 5 + 2 * s))
                    square(2 * i + s)
            act.wait_ge(s_r2, 1)
            nc.scalar.activation(halves(rstd2[:, :]), ps[:, 4:6, 0:HALF], ACT.Sqrt, bias=stat[:, 0:1], scale=1.0 / D
                                 ).then_inc(s_r2s, 1)
            for k in range(KT):
                nc.scalar.copy(xhi[:, k, :], hg[:, k, :]).then_inc(s_n2h, 1)

            def ffn_act(c, last):
                p0 = P_FFN + P_CH * c
                with act.Fori(0, CJ) as j:
                    hi(Unit(p0 + j, 4))
                    hi(Unit(p0 + j, 5))
                    act.wait_ge(s_ev, 2 * p0 + 2 * j + 2)
                    nc.scalar.activation(gt[:, :], gt[:, :], ACT.Silu).then_inc(s_silu, 1)
                    hi(Unit(p0 + j, 6))
                    hi(Unit(p0 + j, 7))
                    act.wait_ge(s_hm, CJ * c + j + 1)
                    nc.scalar.copy(tile_of(hidh, j), halves(ut[:, :])).then_inc(s_hh, 1)
                with act.Fori(0, 7 if last else 8) as i:
                    hi4(p0 + CJ + i)

            with act.Fori(0, CH - 1) as c:
                ffn_act(c, False)
            ffn_act(CH - 1, True)

            for i in range(5):
                act.wait_ge(s_yt, 4 * (i + 1))
                if i == 0:
                    act.wait_ge(s_mm, 2 * M_ALL)
                nc.scalar.activation(junk2[0:tok[i], :], row_banks(i), ACT.Square,
                                     accum_out=stat[0:tok[i], 40 + i:41 + i]).then_inc(s_ys, 1)
                act.wait_ge(s_ys, 2 * i + 1)
                nc.scalar.activation(stat[0:tok[i], 48 + i:49 + i], stat[0:tok[i], 40 + i:41 + i], ACT.Sqrt,
                                     bias=stat[0:tok[i], 0:1], scale=1.0 / D).then_inc(s_ys, 1)

        @block.vector
        def _(dve):
            ve = nc.vector
            ch = Chain(dve, s_dve)

            def lo(u, cols=P):
                dve.wait_ge(s_hi, u.n + 1)
                ve.tensor_tensor(wlo[:, u.slot, :, 0:cols], raw[:, u.slot, :, 0:cols],
                                 whi[:, u.slot, :, 0:cols].bitcast(F32), ALU.subtract).then_inc(s_lo, 1)

            def x_low(n):
                i, kb = divmod(n, 4)
                dve.wait_ge(s_xh, n + 1)
                dst = (slice(None), slice(4 * kb, 4 * kb + 4), slice(P * i, P * i + tok[i]))
                ve.tensor_tensor(xlo[dst], xg[:, n % 2, :, 0:tok[i]], xhi[dst].bitcast(F32), ALU.subtract
                                 ).then_inc(s_xl, 1)

            dve.wait_ge(s_const, 16 * 10)
            dve.wait_ge(s_cc, 2)
            for n in range(20):
                i, kb = divmod(n, 4)
                dve.wait_ge(s_xe, n + 1)
                if n >= 2:
                    dve.wait_ge(s_xl, n - 1)
                ve.tensor_tensor(xg[:, n % 2, :, 0:tok[i]], xT[:, i % 2, 4 * kb:4 * kb + 4, 0:tok[i]],
                                 vec[:, 4 * kb:4 * kb + 4].unsqueeze(2).to_broadcast([P, 4, tok[i]]), ALU.mult
                                 ).then_inc(s_xg, 1)
                if n >= 1:
                    x_low(n - 1)
            x_low(19)
            ve.tensor_copy(identb[:, :], ident[:, :])
            ve.tensor_copy(rowsel[:, :, :], rowselF[:, :, :])
            ve.tensor_copy(biasP[:, 0:P], causF[:, :]).then_inc(s_caus, 1)
            for q in range(4):
                lo(Unit(-1, 2 + q), KIW if q < 2 else P)
            dve.wait_ge(s_rs, 1)
            ch.link(ve.reciprocal(stat[:, 16:21], stat[:, 16:21]))
            for i in range(5):
                ve.tensor_scalar(diag[0:tok[i], i, 0:tok[i]], ident[0:tok[i], 0:tok[i]], stat[0:tok[i], 16 + i:17 + i],
                                 None, ALU.mult).then_inc(s_rd, 1)
            lo(Unit(-1, 6))
            lo(Unit(-1, 7))
            dve.wait_ge(s_rb, 1)
            ve.tensor_copy(rstd1[:, 0:SEQ], ps[:, 4, :])
            ch.link(ve.tensor_copy(rstd1[:, SEQ:NT], ps[:, 5, 0:NS]))
            ch.link(ve.tensor_tensor(tab[:, :, :], tab[:, :, :], rstd1[:, :].unsqueeze(1).to_broadcast([P, 4, NT]),
                                     ALU.mult))
            rs2 = halves(rstd1[:, :])
            c1, s1, c2, s2 = (halves(tab[:, n, :]) for n in range(4))
            rt2 = halves(rt[:, :])

            dve.wait_ge(s_mm, 2)
            ki2 = halves(kiT[:, :])
            ve.tensor_tensor(ki2[0:64], acc(1, 0, 64), c2[0:64], ALU.mult)
            ve.tensor_tensor(rt2[0:32], acc(1, 32, 64), s2[0:32], ALU.mult)
            ve.tensor_tensor(rt2[32:64], acc(1, 0, 32), s2[32:64], ALU.mult)
            ve.tensor_tensor(halves(wT[:, :]), acc(1, 64, 80), rs2[0:16], ALU.mult).then_inc(s_ev, 1)
            dve.wait_ge(s_ev, 1)
            ch.link(ve.tensor_tensor(kiT[0:64, :], kiT[0:64, :], rt[0:64, :], ALU.add))
            ve.tensor_copy(kiT[64:128, :], kiT[0:64, :]).then_inc(s_proj, 1)

            def rope(dst, slot, m, before, cos, sin, width):
                dve.wait_ge(s_proj, before)
                ve.tensor_tensor(dst, acc(slot), cos, ALU.mult)
                r = width // 2
                for p0 in range(0, P, r):
                    q0 = p0 + r if p0 // r % 2 == 0 else p0 - r
                    ins = ve.tensor_tensor(rt2[p0:p0 + r], acc(slot, q0, q0 + r), sin[p0:p0 + r], ALU.mult)
                ins.then_inc(s_ev, 1)
                dve.wait_ge(s_ev, m + 1)
                ve.tensor_tensor(dst, dst, rt2, ALU.add).then_inc(s_proj, 1)

            def pair(p, first, second, mid=None):
                lo(Unit(p, 4))
                lo(Unit(p, 5))
                dve.wait_ge(s_mm, 4 * p + 4)
                first()
                if mid:
                    mid()
                lo(Unit(p, 6))
                lo(Unit(p, 7))
                dve.wait_ge(s_mm, 4 * p + 6)
                second()

            def rope_pair(p, dst, j, before, cos, sin, width):
                pair(p, lambda: rope(tile_of(dst, j), 0, 2 * p + 1, before, cos, sin, width),
                     lambda: rope(tile_of(dst, j + 1), 1, 2 * p + 2, before + 1, cos, sin, width))

            dve.wait_ge(s_sp[0], 48)
            dve.wait_ge(s_sp[1], 32)
            with dve.Fori(0, 4) as i:
                rope_pair(P_QI + i, qT, 2 * i, 1 + 2 * i, c2, s2, ID)

            dve.wait_ge(s_wt, 1)
            ve.tensor_scalar(wiP[:, :, :], ps[:, 7, 0:64].rearrange("p (i h) -> p i h", i=4), ISCALE, None, ALU.mult
                             ).then_inc(s_wtc, 1)
            dve.wait_ge(s_wtc, 1)
            n = 0
            for i in range(1, 4):
                for hh in range(IH):
                    dve.wait_ge(s_ir, n + 1)
                    dst = scP[:, SO[i]:SO[i] + SW[i]]
                    if hh == 0:
                        ve.tensor_scalar(dst, rel[:, n % 2, 0:SW[i]], wiP[:, i, 0:1], None, ALU.mult).then_inc(s_ia, 1)
                    else:
                        dve.wait_ge(s_ia, n)
                        ve.scalar_tensor_tensor(dst, rel[:, n % 2, 0:SW[i]], wiP[:, i, hh:hh + 1], dst,
                                                ALU.mult, ALU.add).then_inc(s_ia, 1)
                    n += 1
            dve.wait_ge(s_proj, 9)
            ve.memset(wsel[:, :, :, :], 0.0)
            ch.link(ve.memset(qiS[:, :, :, :, :], 0.0))
            for half in range(2):
                for src in range(2):
                    ve.tensor_copy(qiS[64 * half:64 * half + 64, :, half, src::2, :].rearrange("p b j t -> p j b t"),
                                   qT[64 * src:64 * src + 64, :, SEQ:NT].rearrange("p j (b t) -> p j b t", t=T))
            dve.wait_ge(s_wt, 2)
            dve.wait_ge(s_const, 16 * NCONST)
            for par in range(2):
                r = slice(64 * par, 64 * par + 64)
                for b in range(B):
                    last = ve.scalar_tensor_tensor(wsel[r, b, par, T * b:T * b + T], ps[r, 7, T * b:T * b + T],
                                                   ISCALE, tsel[r, T * b:T * b + T], ALU.mult, ALU.mult)
            last.then_inc(s_wtc, 1)

            def topk_waits(count):
                dve.wait_ge(s_topk, count)
                ve.tensor_copy(stat[:, 61:62], stat[:, 60:61])

            dve.wait_ge(s_pool, 6)
            with dve.Fori(0, KP_ // 8) as r:
                for i in range(1, 4):
                    ve.max(m8[:, i, :], scP[:, SO[i]:SO[i] + SW[i]]).then_inc(s_topk, 1)
                topk_waits(6 * r + 3)
                for i in range(1, 4):
                    v = scP[:, SO[i]:SO[i] + SW[i]]
                    ve.match_replace(v, m8[:, i, :], v, TAKEN).then_inc(s_topk, 1)
                topk_waits(6 * r + 6)
            for i in range(1, 4):
                last = ve.tensor_scalar(biasP[:, BO[i]:BO[i] + SW[i]], scP[:, SO[i]:SO[i] + SW[i]],
                                        0.5 * (INVALID + TAKEN), MASKED, ALU.is_gt, ALU.mult)
            last.then_inc(s_bias, 1)

            dve.wait_ge(s_hs, 3 * B)
            for par in range(2):
                for hf in range(2):
                    dst = scS[:, 0:PAST].rearrange("p (k r n) -> p k r n", r=2, n=P)[:, 4 * hf:4 * hf + 4, par, :]
                    ve.tensor_copy(dst, ps[NS * par:NS * par + NS, hf, :].rearrange("p (k n) -> p k n", k=4))
            ch.link(ve.tensor_tensor(scS[:, PAST:NSK], ps[0:NS, 4, 0:NS], tailm[:, :], ALU.add))
            ve.memset(gbuf[:, 0:CK - 1], 0.0).then_inc(s_xs, 1)

            gs = gbuf[:, SEQ + CK - 1:].rearrange("p (b s) -> p b s", b=B)

            def taps(c, k0, k1):
                yp = y[:, bass.ds(c, 1), 0:SEQ].rearrange("p a n -> p (a n)")
                ys = y[:, bass.ds(c, 1), SEQ:NT].rearrange("p a (b t) -> p (a b) t", b=B)
                for k in range(k0, k1):
                    wk = cw[:, bass.ds(c, 1), k]
                    for s, (dst, src) in enumerate(((yp, gbuf[:, k:k + SEQ]), (ys, gs[:, :, k:k + T]))):
                        if k == 0:
                            ve.tensor_scalar(dst, src, wk, vec[:, bass.ds(32 + c, 1)], ALU.mult, ALU.add
                                             ).then_inc(s_conv, 1)
                        else:
                            dve.wait_ge(s_conv, 2 * CK * c + 2 * k - 1 + s)
                            ve.scalar_tensor_tensor(dst, src, wk, dst, ALU.mult, ALU.add).then_inc(s_conv, 1)

            def gated(c):
                if not (isinstance(c, int) and c == 0):
                    dve.wait_ge(s_conv, 2 * CK * c)
                ve.tensor_copy(gs[:, :, 0:CK - 1], stT[:, bass.ds(c, 1), :].rearrange("p a (b s) -> p (a b) s", b=B))
                dve.wait_ge(s_sg, c + 1)
                ve.tensor_tensor(gbuf[:, CK - 1:CK - 1 + SEQ], ga[:, 0:SEQ], sg[:, 0:SEQ], ALU.mult)
                ch.link(ve.tensor_tensor(gs[:, :, CK - 1:], ga[:, SEQ:].rearrange("p (b t) -> p b t", b=B),
                                         sg[:, SEQ:].rearrange("p (b t) -> p b t", b=B), ALU.mult))
                if not (isinstance(c, int) and c == 0):
                    dve.wait_ge(s_tt, c)
                ve.tensor_copy(tg[:, 0:CK - 1], gbuf[:, SEQ:SEQ + CK - 1])
                ve.tensor_copy(tg[:, CK - 1:CK - 1 + NS].rearrange("p (b t) -> p b t", b=B), gs[:, :, CK - 1:]).then_inc(s_tg, 1)

            def plain(dst, slot):
                ve.tensor_tensor(dst, acc(slot), rs2, ALU.mult).then_inc(s_ev, 1)

            def topk_sample(rounds, base):
                with dve.Fori(0, rounds) as r:
                    topk_round(base + 2 * r)

            def topk_round(base):
                ve.max(m8[0:NS, 0, :], scS[:, :]).then_inc(s_topk, 1)
                topk_waits(base + 1)
                ve.match_replace(scS[:, :], m8[0:NS, 0, :], scS[:, :], TAKEN).then_inc(s_topk, 1)
                topk_waits(base + 2)

            def u_step(c, conv):
                pair(P_U + c, lambda: plain(halves(ga[:, :]), 0), lambda: plain(halves(sg[:, :]), 1),
                     mid=(lambda: taps(c - 1, 0, 16)) if conv else None)
                if conv:
                    taps(c - 1, 16, CK)
                gated(c)
                topk_round(T0 + 2 * c)

            dve.wait_ge(s_stc, CT)
            dve.wait_ge(s_kio, 32)
            ch.link(ve.memset(tg[:, :], 0.0))
            T0 = 6 * (KP_ // 8)
            u_step(0, False)
            with ch.loop(1, CT, 1) as c:
                u_step(c, True)
            taps(CT - 1, 0, CK)
            T0 += 2 * CT
            with dve.Fori(0, 4) as i:
                rope_pair(P_Q + i, qT, 2 * i, 9 + 2 * i, c1, s1, HD)
                topk_sample(4, T0 + 8 * i)
            T0 += 32
            rope_pair(P_K, kT, 0, 17, c1, s1, HD)
            topk_sample(4, T0)
            T0 += 8
            pair(P_V, lambda: plain(tile_of(vT, 0), 0), lambda: plain(tile_of(vT, 1), 1))
            topk_sample(4, T0)
            assert T0 + 8 == 6 * (KP_ // 8) + 2 * (KS_ // 8)
            dve.wait_ge(s_cvo, 48)
            ve.tensor_scalar(biasS[:, :], scS[:, :], 0.5 * (INVALID + TAKEN), MASKED, ALU.is_gt, ALU.mult
                             ).then_inc(s_bias, 1)
            for kv in range(NKV):
                last = ve.tensor_copy(
                    qpad[:, :, kv, 16 * kv:16 * kv + 16].rearrange("p b (g t) -> p g b t", g=GRP),
                    qT[:, GRP * kv:GRP * kv + GRP, SEQ:NT].rearrange("p g (b t) -> p g b t", b=B))
            last.then_inc(s_qp, 1)
            dve.wait_ge(s_l1, 1)
            ch.link(ve.tensor_scalar(halves(mu[:, :]), ps[:, 6:8, 0:HALF], 1.0 / CW_, None, ALU.mult))
            for c in range(CT):
                ve.tensor_tensor(y[:, c, :], y[:, c, :], mu[:, :], ALU.subtract).then_inc(s_yc, 1)
            dve.wait_ge(s_sd, 1)
            ch.link(ve.reciprocal(rl[:, :], rl[:, :]))
            for c in range(CT + 1):
                if c < CT:
                    ve.tensor_tensor(y[:, c, :], y[:, c, :], rl[:, :], ALU.mult).then_inc(s_yn, 1)
                if c >= 1:
                    dve.wait_ge(s_yh, 2 * c)
                    ve.tensor_tensor(xlo[:, 7 + c, :], y[:, c - 1, :], xhi[:, 7 + c, :].bitcast(F32), ALU.subtract
                                     ).then_inc(s_mix, 1)

            for x in range(32 + 4):
                if x < 32:
                    w = SW[x // 8]
                    dve.wait_ge(s_s, x + 1)
                    if x >= 4:
                        dve.wait_ge(s_p, x - 3)
                    ve.reduce_max(stat[:, 36 + x % 4:37 + x % 4], ps[:, (4, 5, 0, 1)[x % 4], 0:w], AX.X
                                  ).then_inc(s_nm2, 1)
                    dve.wait_ge(s_nm2, x + 1)
                    ve.tensor_scalar(stat[:, 24 + x % 4:25 + x % 4], stat[:, 36 + x % 4:37 + x % 4], -ASCALE, None,
                                     ALU.mult).then_inc(s_nm, 1)
                if 0 <= x - 1 < 32:
                    z = x - 1
                    dve.wait_ge(s_p, z + 1)
                    ch.link(ve.reciprocal(stat[:, 28 + z % 4:29 + z % 4], stat[:, 28 + z % 4:29 + z % 4]))
                    ve.tensor_scalar(pP[:, z % 3, 0:SW[z // 8]], pP[:, z % 3, 0:SW[z // 8]],
                                     stat[:, 28 + z % 4:29 + z % 4], None, ALU.mult).then_inc(s_pn, 1)
                if x >= 4 and (x - 4) % 4 == 3:
                    z = x - 4
                    dve.wait_ge(s_oh, z // 4 + 1)
                    h0, q0 = z % 8 - 3, P * (z // 8)
                    ve.tensor_tensor(xlo[:, h0:h0 + 4, q0:q0 + P],
                                     ps[:, (7, 3)[z // 4 % 2], :].rearrange("p (k n) -> p k n", k=4),
                                     xhi[:, h0:h0 + 4, q0:q0 + P].bitcast(F32), ALU.subtract).then_inc(s_ol, 1)

            for g in range(2):
                for q in range(16 * g, 16 * g + 16):
                    dve.wait_ge(s_chunk, 16 * g + q + 1)
                    if q >= 2:
                        dve.wait_ge(s_ks, q - 1)
                    ve.tensor_copy(kpT[:, q % 2, 1, :], ps[:, 6, :]).then_inc(s_kcd, 1)
                dve.wait_ge(s_gb, g + 1)
                ch.link(ve.reduce_max(stat[:, 34:35], score_row, AX.X))
                ve.tensor_scalar(stat[:, 32:33], stat[:, 34:35], -ASCALE, None, ALU.mult).then_inc(s_gm, 1)
                dve.wait_ge(s_gp, g + 1)
                ch.link(ve.reciprocal(stat[:, 33:34], stat[:, 33:34]))
                ve.tensor_scalar(pS[:, :], pS[:, :], stat[:, 33:34], None, ALU.mult).then_inc(s_gn, 1)
                for kv in range(NKV):
                    dve.wait_ge(s_gh, 2 * g + kv + 1)
                    ve.tensor_tensor(mixed(xlo, kv, g), pv_bank(kv), mixed(xhi, kv, g).bitcast(F32),
                                     ALU.subtract).then_inc(s_gl, 1)

            ve.memset(sqa[:, :], 0.0).then_inc(s_sqs, 1)
            dve.wait_ge(s_sqs, 1)

            def residual(j, s, count):
                dve.wait_ge(s_xr[s], count)
                ve.tensor_tensor(tile_of(h, j), acc(s), halves(xTr[:, s, :]), ALU.add).then_inc(s_ev, 1)
                dve.wait_ge(s_ev, M_OUT + j + 1)
                ve.tensor_scalar(tile_of(hg, j), tile_of(h, j), vec[:, bass.ds(16 + j, 1)], None, ALU.mult
                                 ).then_inc(s_h, 1)
                dve.wait_ge(s_sqh, j + 1)
                ve.tensor_tensor(sqa[:, :], sqa[:, :], sq2[:, :], ALU.add).then_inc(s_sqs, 1)
                dve.wait_ge(s_sqs, j + 2)

            with dve.Fori(0, 8) as i:
                pair(P_OUT + i, lambda: residual(2 * i, 0, 16 * i + 16), lambda: residual(2 * i + 1, 1, 16 * i + 16))
            for k in range(KT):
                dve.wait_ge(s_n2h, k + 1)
                ve.tensor_tensor(xlo[:, k, :], hg[:, k, :], xhi[:, k, :].bitcast(F32), ALU.subtract).then_inc(s_n2, 1)
            dve.wait_ge(s_r2s, 1)
            ch.link(ve.reciprocal(rstd2[:, :], rstd2[:, :]))

            r22 = halves(rstd2[:, :])

            def ffn_dve(c, last):
                p0 = P_FFN + P_CH * c

                def up(j):
                    ve.tensor_tensor(halves(ut[:, :]), acc(1), r22, ALU.mult).then_inc(s_ev, 1)
                    dve.wait_ge(s_ev, 2 * (p0 + j) + 3)
                    dve.wait_ge(s_silu, CJ * c + j + 1)
                    ve.tensor_tensor(ut[:, :], ut[:, :], gt[:, :], ALU.mult).then_inc(s_hm, 1)
                    dve.wait_ge(s_hh, CJ * c + j + 1)
                    ve.tensor_tensor(tile_of(hidl, j), halves(ut[:, :]), tile_of(hidh, j).bitcast(F32), ALU.subtract
                                     ).then_inc(s_hid, 1)
                    dve.wait_ge(s_hid, CJ * c + j + 1)

                with dve.Fori(0, CJ) as j:
                    pair(p0 + j,
                         lambda: ve.tensor_tensor(halves(gt[:, :]), acc(0), r22, ALU.mult).then_inc(s_ev, 1),
                         lambda: up(j))

                def add(j, s):
                    ve.tensor_tensor(tile_of(h, j), acc(s), tile_of(h, j), ALU.add).then_inc(s_ev, 1)

                with dve.Fori(0, 7 if last else 8) as i:
                    pair(p0 + CJ + i, lambda: add(2 * i, 0), lambda: add(2 * i + 1, 1))
                if last:
                    for s in range(2):
                        dve.wait_ge(s_mm, 2 * M_ALL - 2 + 2 * s)
                        add(14 + s, s)

            with dve.Fori(0, CH - 1) as c:
                ffn_dve(c, False)
            ffn_dve(CH - 1, True)

            dve.wait_ge(s_gf, 16)
            for i in range(5):
                dve.wait_ge(s_ys, 2 * i + 2)
                if i >= 2:
                    dve.wait_ge(s_yo[i % 2], 16 * (i // 2))
                ch.link(ve.reciprocal(stat[0:tok[i], 48 + i:49 + i], stat[0:tok[i], 48 + i:49 + i]))
                ve.scalar_tensor_tensor(yo[0:tok[i], i % 2, :], row_banks(i), stat[0:tok[i], 48 + i:49 + i],
                                        gfb[0:tok[i], :], ALU.mult, ALU.mult).then_inc(s_yd, 1)

        @block.tensor
        def _(pe):
            te = nc.tensor

            def unit(u, slot, hf, k=UK, k0=0, cols=P, xh=xhi, xl=xlo):
                pe.wait_ge(s_lo, u.n + 1)
                for t in range(k):
                    for w, x in ((whi, xh), (whi, xl), (wlo, xh)):
                        for half in range(2):
                            ins = te.matmul(ps[0:cols, 2 * slot + half, 0:HALF], w[:, u.slot, t, 0:cols],
                                            x[:, k0 + t, HALF * half:HALF * half + HALF],
                                            start=(hf == 0 and t == 0 and w is whi and x is xh),
                                            stop=(hf == 1 and t == k - 1 and w is wlo))
                ins.then_inc(s_mm, 1)

            def tile(p, s):
                if not (isinstance(p, int) and p == 0 and s == 0):
                    pe.wait_ge(s_ev, 2 * p + s)
                for hf in range(2):
                    unit(Unit(p, 2 * s + hf), s, hf, k0=UK * hf)

            def pair(p):
                tile(p, 0)
                tile(p, 1)

            pe.wait_ge(s_const, 16 * 10)
            te.transpose(ps[:, 0, 0:56], vecN[:, :], ident[0:56, 0:56])
            for c in range(CT):
                ins = te.transpose(ps[:, 1, CK * c:CK * c + CK], cwN[:, P * c:P * c + P], ident[0:CK, 0:CK])
            ins.then_inc(s_ct, 1)
            for i in range(5):
                r = tok[i]
                pe.wait_ge(s_xn[i % 2], 16 * (i // 2 + 1))
                for kb in range(4):
                    if i >= 1:
                        pe.wait_ge(s_xe, 4 * (i - 1) + kb + 1)
                    for k in range(4):
                        ins = te.transpose(ps[:, 4 + kb, P * k:P * k + r],
                                           xN[0:r, i % 2, P * (4 * kb + k):P * (4 * kb + k) + P], ident[0:r, 0:r])
                    ins.then_inc(s_xt, 1)
            pe.wait_ge(s_xl, 20)
            pe.wait_ge(s_cc, 2)
            for hf in range(2):
                unit(Unit(-1, 2 + hf), 1, hf, k0=UK * hf, cols=KIW)
            pe.wait_ge(s_pool, 1)
            pe.wait_ge(s_rd, 5)
            pe.wait_ge(s_xe, 20)
            for i in range(4):
                te.matmul(ps[:, 4, P * i:P * i + P], ones[:, :], diag[:, i, :], start=True, stop=True)
            te.matmul(ps[:, 5, 0:NS], ones[0:NS, :], diag[0:NS, 4, 0:NS], start=True, stop=True).then_inc(s_rb, 1)
            with pe.Fori(0, 4) as i:
                pair(P_QI + i)

            pe.wait_ge(s_proj, 1)
            for i in range(4):
                ins = te.transpose(ps[:, 7, IH * i:IH * i + IH], wT[:, P * i:P * i + P], ident[0:IH, 0:IH])
            ins.then_inc(s_wt, 1)
            pe.wait_ge(s_proj, 9)
            pe.wait_ge(s_wtc, 1)
            n = 0
            for i in range(1, 4):
                for hh in range(IH):
                    if n >= 4:
                        pe.wait_ge(s_ir, n - 3)
                    p0 = 64 * (hh % 2)
                    te.matmul(ps[:, 4 + n % 4, 0:SW[i]], qT[p0:p0 + 64, hh // 2, P * i:P * i + P],
                              kiT[p0:p0 + 64, 0:SW[i]], start=True, stop=True).then_inc(s_is, 1)
                    n += 1
            pe.wait_ge(s_ir, 3 * IH)
            for i in range(4):
                te.transpose(ps[:, 4, ID * i:ID * i + ID], kiT[0:64, P * i:P * i + P], ident[0:64, 0:64])
            te.transpose(ps[0:NS, 5, 0:ID], kiT[0:64, SEQ:NT], ident[0:64, 0:64]).then_inc(s_nt, 1)
            pe.wait_ge(s_const, 16 * NCONST)
            te.matmul(ps[:, 7, 0:NS], hsel[:, :], wT[:, SEQ:NT], start=True, stop=True).then_inc(s_wt, 1)
            pe.wait_ge(s_nc, 1)
            pe.wait_ge(s_ev, M_U)
            pe.wait_ge(s_wtc, 2)

            def head_sum(n):
                b, c = divmod(n, 3)
                pe.wait_ge(s_dr, n + 1)
                if c < 2:
                    te.matmul(ps[0:2 * NS, c, :], wsel[:, b, :, :].rearrange("p r n -> p (r n)"), rel[:, n % 2, :],
                              start=(b == 0), stop=(b == B - 1)).then_inc(s_hs, 1)
                else:
                    te.matmul(ps[0:NS, 4, 0:NS], wsel[0:64, b, 0, :], rel[0:64, n % 2, 0:NS],
                              start=(b == 0), stop=(b == B - 1)).then_inc(s_hs, 1)

            for b in range(B):
                pe.wait_ge(s_ik[b % IB], 16 * (NPG if b < IB else NPG + NPG // 2))
                if b >= IB:
                    pe.wait_ge(s_iks[b % IB], 16 * (NPG // 2))
                for g in range(2):
                    if b or g:
                        pe.wait_ge(s_ic, 2 * b + g)
                    for k in range(4):
                        q = 8 * g + 2 * k
                        ins = te.transpose(ps[:, 5, P * k:P * k + P],
                                           idxN[:, b % IB, q:q + 2, :].rearrange("p a d -> p (a d)"), ident[:, :])
                    ins.then_inc(s_it, 1)
                pe.wait_ge(s_ic, 2 * b + 2)
                for c in range(3):
                    n = 3 * b + c
                    if n >= 2:
                        pe.wait_ge(s_dr, n - 1)
                    if c < 2:
                        te.matmul(ps[:, 6 + n % 2, :], qiS[:, b, :, :, :].rearrange("p r h t -> p (r h t)"),
                                  idxT[:, b % 2, 4 * c:4 * c + 4, :].rearrange("p k n -> p (k n)"),
                                  start=True, stop=True).then_inc(s_dt, 1)
                    else:
                        te.matmul(ps[0:64, 6 + n % 2, 0:NS], qiS[0:64, b, 0, :, :].rearrange("p h t -> p (h t)"),
                                  kiT[0:64, SEQ:NT], start=True, stop=True).then_inc(s_dt, 1)
                    if n >= 1:
                        head_sum(n - 1)
            head_sum(3 * B - 1)
            pe.wait_ge(s_st, 16)
            pe.wait_ge(s_xs, 1)
            for c in range(CT):
                if c >= 4:
                    pe.wait_ge(s_stc, c - 3)
                for half in range(2):
                    ins = te.transpose(ps[:, 4 + c % 4, 120 * half:120 * half + 120], stN[:, half, P * c:P * c + P],
                                       ident[0:120, 0:120])
                ins.then_inc(s_stt, 1)
            pe.wait_ge(s_stc, CT)

            def new_state(c):
                pe.wait_ge(s_tg, c + 1)
                if not (isinstance(c, int) and c == 0):
                    pe.wait_ge(s_co, c)
                te.transpose(ps[:, 6, 0:P], tg[:, :], ident[:, :]).then_inc(s_tt, 1)

            pair(P_U)
            with pe.Fori(1, CT) as i:
                tile(P_U + i, 0)
                new_state(i - 1)
                tile(P_U + i, 1)
            tile(P_Q, 0)
            new_state(CT - 1)
            tile(P_Q, 1)
            with pe.Fori(1, 4) as i:
                pair(P_Q + i)
            pair(P_K)
            pair(P_V)

            for n, (src, need) in enumerate(((kT, None), (vT, None))):
                if n == 0:
                    pe.wait_ge(s_proj, 1 + 8 + 8 + 2)
                    pe.wait_ge(s_co, CT)
                else:
                    pe.wait_ge(s_ev, M_OUT)
                    pe.wait_ge(s_nc, 2)
                for i in range(5):
                    for kv in range(NKV):
                        r = tok[i]
                        ins = te.transpose(ps[0:r, 4 + i // 2, 256 * (i % 2) + P * kv:256 * (i % 2) + P * kv + P],
                                           src[:, kv, P * i:P * i + r], ident[:, :])
                ins.then_inc(s_nt, 1)
            pe.wait_ge(s_conv, 2 * CK * CT)
            pe.wait_ge(s_nc, 3)
            for half in range(2):
                for c in range(CT):
                    ins = te.matmul(ps[:, 6 + half, 0:HALF], ones[:, :], y[:, c, HALF * half:HALF * half + HALF],
                                    start=(c == 0), stop=(c == CT - 1))
            ins.then_inc(s_l1, 1)
            for c in range(CT):
                pe.wait_ge(s_sqd, c + 1)
                for half in range(2):
                    ins = te.matmul(ps[:, 4 + half, 0:HALF], ones[:, :], sq[:, c % 2, HALF * half:HALF * half + HALF],
                                    start=(c == 0), stop=(c == CT - 1))
                ins.then_inc(s_sqm, 1) if c < CT - 1 else ins.then_inc(s_l2, 1)

            pe.wait_ge(s_bias, 1)
            pe.wait_ge(s_sd, 1)
            pe.wait_ge(s_yc, CT)
            for x in range(32 + 3):
                if x < 32:
                    i, hh = divmod(x, 8)
                    w = SW[i]
                    bank = (4, 5, 0, 1)[x % 4]
                    if x >= 4:
                        pe.wait_ge(s_p, x - 3)
                    te.matmul(ps[:, bank, 0:w], identb[:, :], biasP[:, BO[i]:BO[i] + w], start=True, stop=False)
                    te.matmul(ps[:, bank, 0:w], qT[:, hh, P * i:P * i + P], kT[:, hh // GRP, 0:w],
                              start=False, stop=True).then_inc(s_s, 1)
                if 0 <= x - 2 < 32:
                    z = x - 2
                    pe.wait_ge(s_pn, z + 1)
                    if z >= 2:
                        pe.wait_ge(s_pc, z - 1)
                    for k in range(z // 8 + 1):
                        ins = te.transpose(ps[:, (6, 2)[z % 2], P * k:P * k + P], pP[:, z % 3, P * k:P * k + P],
                                           ident[:, :])
                    ins.then_inc(s_pt, 1)
                if x >= 3:
                    z = x - 3
                    i, hh = divmod(z, 8)
                    pe.wait_ge(s_pc, z + 1)
                    if z % 4 == 0 and z >= 8:
                        pe.wait_ge(s_ol, z // 4 - 1)
                    for k in range(i + 1):
                        ins = te.matmul(ps[:, (7, 3)[z // 4 % 2], P * (z % 4):P * (z % 4) + P],
                                        vN[:, k, P * (hh // GRP):P * (hh // GRP) + P], pPT[:, z % 2, k, :],
                                        start=(k == 0), stop=(k == i))
                    ins.then_inc(s_o, 1)

            pe.wait_ge(s_bias, 2)
            pe.wait_ge(s_qp, 1)
            pe.wait_ge(s_ol, 8)

            def keys(q):
                n = 32 * (q // 16) + q % 16
                pe.wait_ge(s_pg[n % SLOTS], 16 * SPP * (n // SLOTS + 1))
                pe.wait_ge(s_pgp[n % SLOTS], 16 * (4 - SPP) * (n // SLOTS + 1))
                if q >= 1:
                    pe.wait_ge(s_kca, q)
                    pe.wait_ge(s_kcd, q)
                for kv in range(NKV):
                    for k in range(4):
                        ins = te.transpose(ps[:, 5 + kv, P * k:P * k + P], pages[:, n % SLOTS, k, P * kv:P * kv + P],
                                           ident[:, :])
                ins.then_inc(s_chunk, 1)

            for g in range(2):
                if g == 1:
                    pe.wait_ge(s_gl, 2)
                    pe.wait_ge(s_gc, 5)
                for c in range(5):
                    w = 512 if c < 4 else NS
                    te.matmul(ps[:, c, 0:w], rowsel[:, g, :], biasS[:, 512 * c:512 * c + w], start=True, stop=False,
                              skip_group_check=True)
                keys(16 * g)
                for j in range(16):
                    q = 16 * g + j
                    b, c = 4 * g + j // 4, j % 4
                    if j < 15:
                        keys(q + 1)
                    r0 = 32 * (j // 4)
                    pe.wait_ge(s_kca, q + 1)
                    pe.wait_ge(s_kcd, q + 1)
                    for kv in range(NKV):
                        ins = te.matmul(ps[r0:r0 + 32, c, :], qpad[:, b, kv, :], kpT[:, q % 2, kv, :],
                                        start=False, stop=True, skip_group_check=True)
                    ins.then_inc(s_ks, 1)
                    if c == 3:
                        for kv in range(NKV):
                            ins = te.matmul(ps[r0:r0 + 32, 4, 0:NS], qpad[:, b, kv, :], kT[:, kv, SEQ:NT],
                                            start=False, stop=True, skip_group_check=True)
                        if j == 15:
                            ins.then_inc(s_gb, 1)
                pe.wait_ge(s_gn, g + 1)
                for c in range(5):
                    if c >= 2:
                        pe.wait_ge(s_gc, 5 * g + c - 1)
                    if c < 4:
                        for k in range(4):
                            ins = te.transpose(ps[:, 5 + c % 2, P * k:P * k + P],
                                               pS[:, P * (4 * c + k):P * (4 * c + k) + P], ident[:, :])
                    else:
                        ins = te.transpose(ps[0:NS, 5, 0:P], pS[:, PAST:NSK], ident[:, :])
                    ins.then_inc(s_gt, 1)
                pe.wait_ge(s_gc, 5 * g + 5)
                for j in range(16):
                    n = 32 * g + 16 + j
                    r0 = 32 * (j // 4)
                    pe.wait_ge(s_pg[n % SLOTS], 16 * SPP * (n // SLOTS + 1))
                    pe.wait_ge(s_pgp[n % SLOTS], 16 * (4 - SPP) * (n // SLOTS + 1))
                    for k in range(4):
                        for kv in range(NKV):
                            ins = te.matmul(ps[:, (7, 4)[kv], 16 * (j // 4):16 * (j // 4) + 16],
                                            pages[:, n % SLOTS, k, P * kv:P * kv + P],
                                            pST[:, 4 * (j % 4) + k, r0 + 16 * kv:r0 + 16 * kv + 16],
                                            start=(j % 4 == 0 and k == 0), stop=False, skip_group_check=True)
                    if j % 4 == 3:
                        for kv in range(NKV):
                            ins = te.matmul(ps[:, (7, 4)[kv], 16 * (j // 4):16 * (j // 4) + 16],
                                            vN[0:NS, 4, P * kv:P * kv + P],
                                            pST[0:NS, 16, r0 + 16 * kv:r0 + 16 * kv + 16],
                                            start=False, stop=True, skip_group_check=True)
                    ins.then_inc(s_chunk, 1)

            pe.wait_ge(s_gl, 4)
            pe.wait_ge(s_mix, CT)
            with pe.Fori(0, 8) as i:
                pair(P_OUT + i)
            pe.wait_ge(s_sqs, KT + 1)
            for half in range(2):
                ins = te.matmul(ps[:, 4 + half, 0:HALF], ones[:, :], sqa[:, HALF * half:HALF * half + HALF],
                                start=True, stop=True)
            ins.then_inc(s_r2, 1)
            pe.wait_ge(s_n2, KT)

            def ffn_pe(c):
                p0 = P_FFN + P_CH * c
                with pe.Fori(0, CJ) as j:
                    pair(p0 + j)
                with pe.Fori(0, 8) as i:
                    for s in range(2):
                        pe.wait_ge(s_ev, 2 * (p0 + CJ + i) + s)
                        for hf in range(2):
                            pe.wait_ge(s_hid, CJ * c + (DK[0] if hf == 0 else CJ))
                            unit(Unit(p0 + CJ + i, 2 * s + hf), s, hf, k=DK[hf], k0=DK[0] * hf, xh=hidh, xl=hidl)

            with pe.Fori(0, CH) as c:
                ffn_pe(c)

            pe.wait_ge(s_ev, M_ALL)
            for i in range(5):
                if i >= 2:
                    pe.wait_ge(s_yd, i - 1)
                for kb in range(4):
                    for k in range(4):
                        ins = te.transpose(ps[0:tok[i], 4 * (i % 2) + kb, P * k:P * k + P],
                                           h[:, 4 * kb + k, P * i:P * i + tok[i]], ident[:, :])
                    ins.then_inc(s_yt, 1)


_INS = ['x_prompt', 'x_sample', 'cache_k', 'cache_v', 'cache_idx_k', 'state_conv', 'page_table', 'norm_attn', 'w_in',
        'conv_dw', 'conv_dw_bias', 'conv_ln_g', 'conv_ln_b', 'w_out', 'norm_ffn', 'w_gate', 'w_up', 'w_down',
        'norm_final']
_OUTS = [('y_prompt', (1, SEQ, D)), ('y_sample', (B, T, D)), ('k_prompt', (1, 1, SEQ, NKV, HD)),
         ('v_prompt', (1, 1, SEQ, NKV, HD)), ('idx_k_prompt', (1, 1, SEQ, ID)), ('conv_prompt', (1, 1, CK - 1, CW_)),
         ('k_sample', (1, B, T, NKV, HD)), ('v_sample', (1, B, T, NKV, HD)), ('idx_k_sample', (1, B, T, ID)),
         ('conv_sample', (1, B, CK - 1, CW_))]


def constants():
    f32 = np.float32
    pos = np.concatenate([np.arange(SEQ), np.tile(PAST + np.arange(T), B)]).astype(f32)
    rope = np.zeros((P, 4, NT), f32)
    for n, width in ((0, HD), (2, ID)):
        half = width // 2
        expo = (-(np.arange(half, dtype=f32) / f32(half))).astype(np.float64)
        freq = (np.float64(10000.0) ** expo).astype(f32)
        d = np.arange(P) % width
        ang = (pos[None, :] * freq[d % half][:, None]).astype(f32).astype(np.float64)
        rope[:, n] = np.cos(ang)
        rope[:, n + 1] = np.where(d[:, None] < half, -np.sin(ang), np.sin(ang))
    tokens = np.arange(NS)
    row = np.arange(P)
    hsel = (np.arange(IH)[:, None] == row[None, :] // T % IH).astype(f32)
    tsel = (row[:, None] % T == tokens[None, :] % T).astype(f32)
    own = (tokens[:, None] // T == tokens[None, :] // T) & (tokens[None, :] <= tokens[:, None])
    tail = np.where(own, 0.0, INVALID).astype(f32)
    rowsel = np.zeros((NS, 2, P), f32)
    for g in range(2):
        rowsel[T * (4 * g + row // 32) + row % T, g, row] = 1.0
    caus = np.where(row[None, :] <= row[:, None], 0.0, MASKED).astype(f32)
    return {'c_ident': np.eye(P, dtype=f32), 'c_rope': rope, 'c_hsel': hsel, 'c_tsel': tsel, 'c_tail': tail,
            'c_rowsel': rowsel, 'c_caus': caus}


def kernel(**inputs):
    import concourse.bacc as _bacc
    from concourse.bass_utils import run_bass_kernel_spmd as _run

    nc = _bacc.Bacc("TRN2", target_bir_lowering=False, num_devices=1)
    arrays, a, o = {}, {}, {}
    for name, v in [(n, np.ascontiguousarray(inputs[n])) for n in _INS] + list(constants().items()):
        arrays[f"in_{name}"] = v
        a[name] = nc.dram_tensor(f"in_{name}", v.shape, mybir.dt.from_np(v.dtype), kind="ExternalInput").ap()
    for name, shape in _OUTS:
        o[name] = nc.dram_tensor(f"out_{name}", shape, F32, kind="ExternalOutput").ap()
    a['xT_dram'] = nc.dram_tensor("xT_dram", (D, NT), F32, kind="Internal").ap()
    build(nc, a, o)
    r = _run(nc, [arrays], core_ids=[0])
    return tuple(r.results[0][f"out_{name}"] for name, _ in _OUTS)
```

```python
from contextlib import ExitStack, contextmanager

import numpy as np
import concourse.bass as bass
from concourse import mybir

F32 = mybir.dt.float32
F32R = mybir.dt.float32r
BF16 = mybir.dt.bfloat16
I32 = mybir.dt.int32
ALU = mybir.AluOpType
ACT = mybir.ActivationFunctionType
AX = mybir.AxisListType

P = 128
D = 2048
SEQ = 512
B, T = 8, 4
NS = B * T
NT = SEQ + NS
HALF = NT // 2
KT = D // P
NH, NKV, HD = 8, 2, 128
GRP = NH // NKV
IH, ID = 16, 64
PAST, PAGE = 2048, 128
NPG = PAST // PAGE
CW_, CK = 1024, 31
CT = CW_ // P
DFF = 5632
EPS = 1e-6
KP_, KS_ = min(256, SEQ // 4), min(256, (PAST + T) // 4)
INVALID, TAKEN, MASKED = -3.0e38, -3.3e38, -1.0e30
ISCALE = float(ID) ** -0.5 * float(IH) ** -0.5
ASCALE = float(HD) ** -0.5

COL_Q, COL_K, COL_V, COL_QI, COL_KI = 0, 1024, 1280, 1536, 2560
COL_U = COL_KI + ID + IH
KIW = ID + IH

EARLY = 3
LATE = 8
NA = 10
ND = CK - NA
CN = ND + 2
RING = 4
IB = 4
SLOTS, RSLOTS = 16, 12
SPP = 2
UK = 8
CH, CJ = 4, 11
DK = (6, 5)
P_QI = 0
P_U = P_QI + 4
P_Q = P_U + 8
P_K = P_Q + 4
P_V = P_K + 1
P_OUT = P_V + 1
P_FFN = P_OUT + KT // 2
P_CH = CJ + KT // 2
P_ALL = P_FFN + CH * P_CH
M_U, M_OUT, M_FFN, M_ALL = 2 * P_U + 1, 2 * P_OUT + 1, 2 * P_FFN + 1, 2 * P_ALL + 1
NCONST = 6

NSK = PAST + NS
SW = [P * (i + 1) for i in range(4)]
SO = [0, 0, 256, 640]
BO = [0, 128, 384, 768]


class Unit:

    def __init__(self, p, q):
        self.n = 4 * p + 2 + q
        self.slot = (2 + q) % RING
        self.fill = p + (2 + q) // RING + 1
        self.first = isinstance(p, int) and self.n < RING


class Chain:

    def __init__(self, eng, sem):
        self.eng, self.sem, self.n, self.reg = eng, sem, 0, 0

    def link(self, ins):
        ins.then_inc(self.sem, 1)
        self.n += 1
        self.eng.wait_ge(self.sem, self.n + self.reg)

    @contextmanager
    def loop(self, start, end, per):
        n0 = self.n
        with self.eng.Fori(start, end) as i:
            self.reg = per * (i - start)
            yield i
        assert self.n == n0 + per
        self.n, self.reg = n0 + per * (end - start), 0


def build(nc, a, o):
    with ExitStack() as ctx:
        def sem(name):
            return ctx.enter_context(nc.semaphore(name))

        base = -(-nc.sbuf_base // 32) * 32
        ctx.enter_context(nc.sbuf_tensor("fence", [P, 53194], F32))

        def at(name, shape, dt, offset):
            return nc.alloc_sbuf_tensor_at(name, shape, dt, offset=base + offset)

        raw = at("raw", [P, RING, UK, P], F32, 0)
        whi = at("whi", [P, RING, UK, P], F32R, 16384)
        wlo = at("wlo", [P, RING, UK, P], F32R, 32768)
        xhi = at("xhi", [P, KT, NT], F32R, 49152)
        xlo = at("xlo", [P, KT, NT], F32R, 83968)
        C0 = 118784
        ident = at("ident", [P, P], F32, C0)
        ones = at("ones", [P, P], F32, C0 + 512)
        identb = at("identb", [P, P], BF16, C0 + 1024)
        vec = at("vec", [P, 56], F32, C0 + 1280)
        cw = at("cw", [P, CT, CK], F32, C0 + 1504)
        stat = at("stat", [P, 64], F32, C0 + 2496)
        S0 = C0 + 2816
        qT = at("qT", [P, 8, NT], F32, S0)
        kT = at("kT", [P, NKV, NT], F32, S0 + 17408)
        vN = at("vN", [P, 5, 256], F32, S0 + 21760)
        biasS = at("biasS", [NS, NSK], BF16, S0 + 26880)
        biasP = at("biasP", [P, 1280], BF16, S0 + 31040)
        qpad = at("qpad", [P, B, NKV, 32], F32, S0 + 33600)
        wiP = at("wiP", [P, 4, IH], F32, S0 + 35648)
        rowsel = at("rowsel", [NS, 2, P], BF16, S0 + 35904)
        tab = at("tab", [P, 4, NT], F32, S0 + 36672)
        rstd1 = at("rstd1", [P, NT], F32, S0 + 45376)
        kiT = at("kiT", [P, NT], F32, S0 + 47552)
        scP = at("scP", [P, 1152], F32, S0 + 49728)
        scS = at("scS", [NS, NSK], F32, S0 + 54336)
        R0 = S0 + 62656
        xN = at("xN", [P, 2, D], F32, R0)
        xg = at("xg", [P, 2, 4, P], F32, R0 + 16384)
        rowselF = at("rowselF", [NS, 2, P], F32, R0 + 20480)
        causF = at("causF", [P, P], F32, R0 + 21504)
        xT = at("xT", [P, 2, KT, P], F32, S0)
        junk = at("junk", [P, D], F32, S0 + 17408)
        vecN = at("vecN", [56, P], F32, S0 + 25600)
        cwN = at("cwN", [CK, CW_], F32, S0 + 26112)
        diag = at("diag", [P, 5, P], F32, S0 + 49728)
        idxN = at("idxN", [P, IB, NPG, ID], F32, R0)
        idxT = at("idxT", [P, 2, NPG // 2, P], F32, R0 + 16384)
        kiN = at("kiN", [P, 5, ID], F32, R0 + 24576)
        rel = at("rel", [P, 2, 512], F32, S0 + 17408)
        wT = at("wT", [IH, NT], F32, S0 + 21760)
        qiS = at("qiS", [P, B, 2, IH, T], F32, S0 + 23936)
        wsel = at("wsel", [P, B, 2, NS], F32, S0 + 28032)
        hsel = at("hsel", [IH, P], F32, S0 + 30080)
        tsel = at("tsel", [P, NS], F32, S0 + 30592)
        tailm = at("tailm", [NS, NS], F32, S0 + 30720)
        rt = at("rt", [P, NT], F32, R0 + 23936)
        gbuf = at("gbuf", [P, SEQ + CK - 1 + B * (CK - 1 + T)], F32, R0)
        y = at("y", [P, CT, NT], F32, R0 + 3264)
        ga = at("ga", [P, NT], F32, R0 + 20672)
        sg = at("sg", [P, NT], F32, R0 + 22848)
        tg = at("tg", [P, P], F32, R0 + 26112)
        stN = at("stN", [120, 2, CW_], F32, S0)
        stT = at("stT", [P, CT, B * (CK - 1)], F32, S0 + 8192)
        cout = at("cout", [CK - 1 + NS, CW_], F32, S0 + 26880)
        tapS = at("tapS", [P, B, T, CK], F32, S0 + 17408)
        y2 = at("y2", [P, SEQ], F32, S0 + 21760)
        y3 = at("y3", [P, SEQ], F32, S0 + 23936)
        tap = at("tap", [P, 2, SEQ], F32, S0 + 49728)
        vT = at("vT", [P, NKV, NT], F32, S0 + 49728)
        kN = at("kN", [P, 5, 256], F32, S0 + 38848)
        mu = at("mu", [P, NT], F32, S0 + 21760)
        rl = at("rl", [P, NT], F32, S0 + 23936)
        sq = at("sq", [P, 2, NT], F32, S0 + 49728)
        pP = at("pP", [P, 3, SEQ], F32, S0 + 36672)
        pPT = at("pPT", [P, 2, 4, P], F32, S0 + 42816)
        ring_pages = at("ring_pages", [P, RSLOTS, 4, 256], F32, 0)
        own_pages = at("own_pages", [P, SLOTS - RSLOTS, 4, 256], F32, R0)
        kpT = at("kpT", [P, 2, NKV, 512], F32, R0 + 16384)
        pS = at("pS", [P, NSK], F32, S0 + 36672)
        pST = at("pST", [P, 17, P], F32, S0 + 44992)
        oS = at("oS", [P, 256], F32, S0 + 36672)
        h = at("h", [P, KT, NT], F32, S0)
        hidh = at("hidh", [P, CJ, NT], F32R, S0 + 34816)
        hidl = at("hidl", [P, CJ, NT], F32R, S0 + 58752)
        gt = at("gt", [P, NT], F32, S0 + 82688)
        ut = at("ut", [P, NT], F32, S0 + 84864)
        rstd2 = at("rstd2", [P, NT], F32, S0 + 87040)
        hg = at("hg", [P, KT, NT], F32, S0 + 34816)
        xTr = at("xTr", [P, 2, NT], F32, S0 + 69632)
        sq2 = at("sq2", [P, NT], F32, S0 + 73984)
        sqa = at("sqa", [P, NT], F32, S0 + 76160)
        gfb = at("gfb", [P, D], F32, S0 + 34816)
        yo = at("yo", [P, 2, D], F32, S0 + 43008)
        junk2 = at("junk2", [P, D], F32, S0 + 59392)

        page = at("page", [P, B * NPG], I32, S0 + 35904)[64:65, :]
        m8 = at("m8", [P, 4, 8], F32, S0 + 36416)
        ps = ctx.enter_context(nc.psum_tensor("ps", [P, 8, 512], F32))

        s_raw = [sem(f"s_raw{i}") for i in range(RING)]
        s_hi, s_lo = sem("s_hi"), sem("s_lo")
        s_mm = sem("s_mm")
        s_ev = sem("s_ev")
        s_proj = sem("s_proj")
        s_vec, s_const = sem("s_vec"), sem("s_const")
        s_ct, s_cc = sem("s_ct"), sem("s_cc")
        s_xn = [sem("s_xn0"), sem("s_xn1")]
        s_xt, s_xe, s_xg, s_xh, s_xl = sem("s_xt"), sem("s_xe"), sem("s_xg"), sem("s_xh"), sem("s_xl")
        s_ssq = sem("s_ssq")
        s_sp = [sem("s_sp0"), sem("s_sp1")]
        s_rs, s_rd, s_rb = sem("s_rs"), sem("s_rd"), sem("s_rb")
        s_dve, s_pool = sem("s_dve"), sem("s_pool")
        s_wt, s_wtc = sem("s_wt"), sem("s_wtc")
        s_is, s_ir, s_ia = sem("s_is"), sem("s_ir"), sem("s_ia")
        s_caus = sem("s_caus")
        s_page = sem("s_page")
        s_ik = [sem(f"s_ik{i}") for i in range(IB)]
        s_iks = [sem(f"s_iks{i}") for i in range(IB)]
        s_it, s_ic = sem("s_it"), sem("s_ic")
        s_dt, s_dr, s_hs, s_xs = sem("s_dt"), sem("s_dr"), sem("s_hs"), sem("s_xs")
        s_st, s_stt, s_stc = sem("s_st"), sem("s_stt"), sem("s_stc")
        s_sg, s_conv, s_tg, s_tt, s_co = sem("s_sg"), sem("s_conv"), sem("s_tg"), sem("s_tt"), sem("s_co")
        s_tap, s_add = sem("s_tap"), sem("s_add")
        s_smul, s_ssum = sem("s_smul"), sem("s_ssum")
        s_topk = sem("s_topk")
        s_bias = sem("s_bias")
        s_nt, s_nc = sem("s_nt"), sem("s_nc")
        s_l1, s_yc, s_sqd, s_sqm, s_l2, s_sd, s_yn, s_yh = (sem("s_" + x) for x in
                                                           ("l1", "yc", "sqd", "sqm", "l2", "sd", "yn", "yh"))
        s_mu, s_rl, s_ysl = sem("s_mu"), sem("s_rl"), sem("s_ysl")
        s_mix = sem("s_mix")
        s_os, s_ot = sem("s_os"), sem("s_ot")
        s_qp = sem("s_qp")
        s_s, s_nm, s_p, s_pn, s_pt, s_pc, s_o, s_oh, s_ol = (sem("s_" + x) for x in
                                                             ("s", "nm", "p", "pn", "pt", "pc", "o", "oh", "ol"))
        s_pg = [sem(f"s_pg{i}") for i in range(SLOTS)]
        s_pgp = [sem(f"s_pgp{i}") for i in range(SLOTS)]
        s_chunk = sem("s_chunk")
        s_kca, s_kcd, s_ks = sem("s_kca"), sem("s_kcd"), sem("s_ks")
        s_gb, s_gm, s_gp, s_gn, s_gt, s_gc, s_gh, s_gl = (sem("s_g" + x) for x in "bmpntchl")
        s_xr = [sem("s_xr0"), sem("s_xr1")]
        s_h, s_sqh, s_sqs = sem("s_h"), sem("s_sqh"), sem("s_sqs")
        s_r2, s_r2s = sem("s_r2"), sem("s_r2s")
        s_n2h, s_n2 = sem("s_n2h"), sem("s_n2")
        s_silu, s_hm, s_hh, s_hid = sem("s_silu"), sem("s_hm"), sem("s_hh"), sem("s_hid")
        s_gf, s_yt, s_ys, s_yd = (sem("s_" + x) for x in ("gf", "yt", "ys", "yd"))
        s_nm2 = sem("s_nm2")
        s_yo = [sem("s_yo0"), sem("s_yo1")]
        s_kio, s_cvo, s_ko, s_vo = sem("s_kio"), sem("s_cvo"), sem("s_ko"), sem("s_vo")

        w_in = a["w_in"][0].rearrange("(t p) n -> p t n", p=P)
        w_out = a["w_out"][0].rearrange("(t p) n -> p t n", p=P)
        w_gate = a["w_gate"][0].rearrange("(t p) n -> p t n", p=P)
        w_up = a["w_up"][0].rearrange("(t p) n -> p t n", p=P)
        w_down = a["w_down"][0].rearrange("(t p) n -> p t n", p=P)
        x_rows = [a["x_prompt"][0][P * i:P * i + P, :] for i in range(4)] + [
            a["x_sample"].rearrange("b t d -> (b t) d")]
        tok = [P] * 4 + [NS]
        xT_dram = a["xT_dram"].rearrange("(t p) n -> p t n", p=P)
        kc = a["cache_k"][0].rearrange("n s k d -> n s (k d)")
        vc = a["cache_v"][0].rearrange("n s k d -> n s (k d)")
        ic = a["cache_idx_k"][0]
        NPOOL = ic.shape[0]

        block = ctx.enter_context(nc.Block())

        def halves(ap):
            return ap.rearrange("p (h n) -> p h n", h=2)

        def tile_of(buf, j):
            return buf[:, bass.ds(j, 1), :].rearrange("p a (h n) -> p (a h) n", h=2)

        def acc(slot, p0=0, p1=P):
            return ps[p0:p1, 2 * slot:2 * slot + 2, 0:HALF]

        flat = ps[:, :, :].rearrange("p b n -> p (b n)")
        score_row = flat[:, 0:NSK]
        gs = gbuf[:, SEQ + CK - 1:].rearrange("p (b s) -> p b s", b=B)

        def row_banks(i):
            return flat[0:tok[i], D * (i % 2):D * (i % 2) + D]

        def pv_bank(kv):
            rows = ps[:, (4, 7)[kv], 0:P].rearrange("p (b v g t) -> p b v g t", b=4, v=NKV, g=GRP)
            return rows[:, :, kv, :, :].rearrange("p b g t -> p g b t")

        def mixed(x, kv, g):
            c0 = SEQ + 4 * T * g
            return x[:, GRP * kv:GRP * kv + GRP, c0:c0 + 4 * T].rearrange("p g (b t) -> p g b t", b=4)

        def rows_out(eng, dst, src, last, width, sem_done):
            eng.copy(dst[:, 0:4, :], src.rearrange("p (i d) -> p i d", i=4))
            eng.copy(dst[0:NS, 4, :], last).then_inc(sem_done, 1)

        def store_rows(eng, prompt, sample, src, sem_done):
            eng.dma_start(prompt.rearrange("(i p) d -> p i d", p=P), src[:, 0:4, :]).then_inc(sem_done, 16)
            eng.dma_start(sample, src[0:NS, 4, :]).then_inc(sem_done, 16)

        def index_pages(eng, b, g0, g1, landed):
            if b >= IB:
                eng.wait_ge(s_it, 2 * (b - IB + 1))
            with eng.Fori(g0, g1) as g:
                pg = eng.value_load(page[0:1, bass.ds(b * NPG + g, 1)], min_val=0, max_val=NPOOL - 1)
                eng.dma_start(idxN[:, b % IB, bass.ds(g, 1), :].rearrange("p a d -> p (a d)"),
                              ic[bass.ds(pg, 1), :, :].rearrange("a s d -> (a s) d")).then_inc(landed[b % IB], 16)

        def page_slot(n):
            s = n % SLOTS
            return ring_pages[:, s, :, :] if s < RSLOTS else own_pages[:, s - RSLOTS, :, :]

        def page_chunks(eng, k0, k1, landed):
            eng.wait_ge(s_page, 16)
            eng.wait_ge(s_mm, 2 * M_OUT)
            for n in range(64):
                g, v, s = n // 32, n // 16 % 2, n % SLOTS
                if n == RSLOTS:
                    eng.wait_ge(s_mix, CT)
                if n >= SLOTS:
                    eng.wait_ge(s_chunk, n - SLOTS + 1)
                for k in range(k0, k1):
                    at0 = 64 * g + 4 * (n % 16) + k
                    pg = eng.value_load(page[0:1, at0:at0 + 1], min_val=0, max_val=NPOOL - 1)
                    eng.dma_start(page_slot(n)[:, k, :],
                                  (kc, vc)[v][bass.ds(pg, 1), :, :].rearrange("a s d -> (a s) d")
                                  ).then_inc(landed[s], 16)

        @block.sync
        def _(sp):
            def load(u, src, k=UK, cols=P):
                if not u.first:
                    sp.wait_ge(s_lo, u.n - RING + 1)
                sp.dma_start(raw[:, u.slot, 0:k, 0:cols], src).then_inc(s_raw[u.slot], 16)

            def col(w, c, hf):
                return w[:, UK * hf:UK * hf + UK, bass.ds(c, P)]

            for i in range(5):
                if i >= 2:
                    sp.wait_ge(s_xt, 4 * (i - 1))
                    sp.wait_ge(s_ssq, i - 1)
                sp.dma_start(xN[0:tok[i], i % 2, :], x_rows[i]).then_inc(s_xn[i % 2], 16)
                if i == 1:
                    sp.wait_ge(s_vec, 16 * 7)
                    for hf in range(2):
                        load(Unit(-1, 2 + hf), w_in[:, UK * hf:UK * hf + UK, COL_KI:COL_KI + KIW], cols=KIW)
                    for hf in range(2):
                        load(Unit(0, hf), col(w_in, COL_QI, hf))
            for hf in range(2):
                load(Unit(0, 2 + hf), col(w_in, COL_QI + P, hf))
            with sp.Fori(1, 4) as i:
                for q in range(4):
                    load(Unit(P_QI + i, q), col(w_in, COL_QI + 256 * i + P * (q // 2), q % 2))
            def conv_input(i):
                for q in range(4):
                    load(Unit(P_U + i, q), col(w_in, COL_U + P * i + CW_ * (q // 2), q % 2))

            conv_input(0)
            sp.wait_ge(s_page, 16)
            for b in range(IB, B):
                index_pages(sp, b, NPG // 2, NPG, s_iks)
            with sp.Fori(1, 8) as i:
                conv_input(i)
            with sp.Fori(0, 4) as i:
                for q in range(4):
                    load(Unit(P_Q + i, q), col(w_in, COL_Q + 256 * i + P * (q // 2), q % 2))
            for q in range(8):
                load(Unit(P_K, q), col(w_in, COL_K + P * (q // 2), q % 2))
            page_chunks(sp, 0, SPP, s_pg)
            def residual(i, s):
                sp.dma_start(xTr[:, s, :], xT_dram[:, bass.ds(2 * i + s, 1), :].rearrange("p a n -> p (a n)")
                             ).then_inc(s_xr[s], 16)

            sp.wait_ge(s_chunk, 64 - SLOTS + RSLOTS)
            for q in range(4):
                load(Unit(P_OUT, q), col(w_out, P * (q // 2), q % 2))
            sp.wait_ge(s_sp[0], 48)
            sp.wait_ge(s_sp[1], 32)
            sp.wait_ge(s_gl, 4)
            for s in range(2):
                residual(0, s)
            with sp.Fori(1, 8) as i:
                for q in range(4):
                    load(Unit(P_OUT + i, q), col(w_out, 256 * i + P * (q // 2), q % 2))
                    if q % 2:
                        sp.wait_ge(s_ev, M_OUT + 2 * i + q // 2 - 1)
                        residual(i, q // 2)
            with sp.Fori(0, CH) as c:
                p0 = P_FFN + P_CH * c
                with sp.Fori(0, CJ) as j:
                    for q in range(4):
                        load(Unit(p0 + j, q), col((w_gate, w_up)[q // 2], P * CJ * c + P * j, q % 2))
                with sp.Fori(0, 8) as i:
                    for q in range(4):
                        hf = q % 2
                        load(Unit(p0 + CJ + i, q),
                             w_down[:, bass.ds(CJ * c + DK[0] * hf, DK[hf]), bass.ds(256 * i + P * (q // 2), P)],
                             k=DK[hf])
            sp.wait_ge(s_mm, 2 * M_ALL)
            sp.dma_start(gfb[:, :], a["norm_final"].partition_broadcast(P)).then_inc(s_gf, 16)
            for i in range(5):
                sp.wait_ge(s_yd, i + 1)
                dst = o["y_prompt"][0][P * i:P * i + P, :] if i < 4 else o["y_sample"].rearrange("b t d -> (b t) d")
                sp.dma_start(dst, yo[0:tok[i], i % 2, :]).then_inc(s_yo[i % 2], 16)
            sp.wait_ge(s_yo[0], 48)
            sp.wait_ge(s_yo[1], 32)
            sp.wait_ge(s_kio, 32)
            sp.wait_ge(s_cvo, 48)
            sp.wait_ge(s_ko, 32)
            sp.wait_ge(s_vo, 32)

        @block.gpsimd
        def _(pool):
            pool.dma_start(ident[:, :], a["c_ident"]).then_inc(s_vec, 16)
            pool.dma_start(vecN[0:16, :], a["norm_attn"][0].rearrange("(k p) -> k p", p=P)).then_inc(s_vec, 16)
            pool.dma_start(vecN[16:32, :], a["norm_ffn"][0].rearrange("(k p) -> k p", p=P)).then_inc(s_vec, 16)
            for n, name in enumerate(("conv_dw_bias", "conv_ln_g", "conv_ln_b")):
                pool.dma_start(vecN[32 + 8 * n:40 + 8 * n, :], a[name][0].rearrange("(k p) -> k p", p=P)
                               ).then_inc(s_vec, 16)
            pool.dma_start(cwN[:, :], a["conv_dw"][0]).then_inc(s_vec, 16)
            pool.dma_start(page, a["page_table"].rearrange("(o b) n -> o (b n)", o=1)).then_inc(s_page, 16)
            pool.dma_start(tab[:, :, :], a["c_rope"]).then_inc(s_const, 16)
            pool.dma_start(rowselF[:, :, :], a["c_rowsel"]).then_inc(s_const, 16)
            pool.dma_start(causF[:, :], a["c_caus"]).then_inc(s_const, 16)
            nc.gpsimd.memset(ones[:, :], 1.0).then_inc(s_pool, 1)
            nc.gpsimd.memset(qpad[:, :, :, :], 0.0).then_inc(s_pool, 1)
            nc.gpsimd.memset(stat[:, :], EPS).then_inc(s_pool, 1)
            c0 = 0
            for i in range(5):
                pool.wait_ge(s_xe, 4 * (i + 1))
                pool.dma_start(xT_dram[:, :, c0:c0 + tok[i]], xT[:, i % 2, :, 0:tok[i]]).then_inc(s_sp[i % 2], 16)
                c0 += tok[i]
            pool.wait_ge(s_xl, 20)
            pool.wait_ge(s_ssq, 5)
            pool.wait_ge(s_caus, 1)
            for dst, name in ((hsel, "c_hsel"), (tsel, "c_tsel"), (tailm, "c_tail")):
                pool.dma_start(dst[:, :], a[name]).then_inc(s_const, 16)

            pool.wait_ge(s_page, 16)
            for b in range(B):
                index_pages(pool, b, 0, NPG if b < IB else NPG // 2, s_ik)
                if b == IB - 1:
                    pool.wait_ge(s_ia, 3 * IH)
                    for i in range(1, 4):
                        v = scP[:, SO[i] + SW[i] - P:SO[i] + SW[i]]
                        nc.gpsimd.affine_select(out=v, in_=v, compare_op=ALU.is_ge, fill=INVALID, base=0,
                                                pattern=[[-1, P]], channel_multiplier=1).then_inc(s_pool, 1)
            pool.wait_ge(s_nc, 1)
            store_rows(pool, o["idx_k_prompt"][0, 0], o["idx_k_sample"][0].rearrange("b t d -> (b t) d"), kiN, s_kio)
            pool.wait_ge(s_hs, 3 * B)
            pool.dma_start(stN[:, :, :], a["state_conv"][0].rearrange("(a b) s c -> (b s) a c", a=2)).then_inc(s_st, 16)
            pool.dma_start(o["conv_sample"][0][:, 0:CK - 1 - T, :], a["state_conv"][0][:, T:CK - 1, :]
                           ).then_inc(s_cvo, 16)
            def low(u):
                pool.wait_ge(s_hi, u.n + 1)
                nc.gpsimd.tensor_tensor(wlo[:, u.slot, :, :], raw[:, u.slot, :, :], whi[:, u.slot, :, :].bitcast(F32),
                                        ALU.subtract).then_inc(s_lo, 1)

            def tap_sums(c, a0, a1):
                for k in range(max(a0, 1), a1):
                    n = (NA - 1) * c + k
                    pool.wait_ge(s_tap, NA * c + k + 1)
                    if k >= 2:
                        pool.wait_ge(s_add, n - 1)
                    nc.gpsimd.tensor_tensor(y2[:, :], y2[:, :], tap[:, (k - 1) % 2, :], ALU.add).then_inc(s_add, 1)

            def sampled_products(c):
                pool.wait_ge(s_tg, c + 1)
                if not (isinstance(c, int) and c == 0):
                    pool.wait_ge(s_ssum, 2 * c)
                for t in range(T):
                    nc.gpsimd.tensor_tensor(tapS[:, :, t, :], gs[:, :, t:t + CK], cw[:, bass.ds(c, 1), :].to_broadcast(
                        [P, B, CK]), ALU.mult).then_inc(s_smul, 1)

            pool.wait_ge(s_lo, 4 * P_U + 6)
            for q in range(4):
                low(Unit(P_U, 4 + q))

            def conv_step(i):
                for q in range(4):
                    if q == 0:
                        sampled_products(i - 1)
                    tap_sums(i - 1, NA * q // 4, NA * (q + 1) // 4)
                    low(Unit(P_U + i, 4 + q))

            conv_step(1)
            with pool.Fori(2, CT + 1) as i:
                conv_step(i)
            pool.wait_ge(s_co, CT)
            pool.dma_start(o["conv_prompt"][0, 0], cout[0:CK - 1, :]).then_inc(s_cvo, 16)
            pool.dma_start(o["conv_sample"][0][:, CK - 1 - T:CK - 1, :], cout[CK - 1:CK - 1 + NS, :]
                           ).then_inc(s_cvo, 16)
            def lows(p):
                for q in range(4):
                    low(Unit(p, 4 + q))

            lows(P_Q + 1)
            pool.wait_ge(s_mu, 1)
            for c in range(CT):
                nc.gpsimd.tensor_tensor(y[:, c, :], y[:, c, :], mu[:, :], ALU.subtract).then_inc(s_yc, 1)
            lows(P_Q + 2)
            pool.wait_ge(s_rl, 1)
            for c in range(CT):
                nc.gpsimd.tensor_tensor(y[:, c, :], y[:, c, :], rl[:, :], ALU.mult).then_inc(s_yn, 1)
            with pool.Fori(P_Q + 3, P_V) as p:
                lows(p)
            pool.wait_ge(s_nc, 2)
            store_rows(pool, o["k_prompt"][0, 0].rearrange("s k d -> s (k d)"),
                     o["k_sample"][0].rearrange("b t k d -> (b t) (k d)"), kN, s_ko)
            pool.wait_ge(s_nc, 3)
            store_rows(pool, o["v_prompt"][0, 0].rearrange("s k d -> s (k d)"),
                     o["v_sample"][0].rearrange("b t k d -> (b t) (k d)"), vN, s_vo)
            page_chunks(pool, SPP, 4, s_pgp)

        @block.scalar
        def _(act):
            def hi(u, cols=P):
                act.wait_ge(s_raw[u.slot], 16 * u.fill)
                if not u.first:
                    act.wait_ge(s_mm, u.n - RING + 1)
                nc.scalar.copy(whi[:, u.slot, :, 0:cols], raw[:, u.slot, :, 0:cols]).then_inc(s_hi, 1)

            def x_high(n):
                i, kb = divmod(n, 4)
                act.wait_ge(s_xg, n + 1)
                nc.scalar.copy(xhi[:, 4 * kb:4 * kb + 4, P * i:P * i + tok[i]], xg[:, n % 2, :, 0:tok[i]]
                               ).then_inc(s_xh, 1)

            act.wait_ge(s_ct, 1)
            nc.scalar.copy(vec[:, :], ps[:, 0, 0:56]).then_inc(s_cc, 1)
            nc.scalar.copy(cw[:, :, :], ps[:, 1, 0:CT * CK].rearrange("p (c k) -> p c k", c=CT)).then_inc(s_cc, 1)
            for i in range(5):
                if i >= 2:
                    act.wait_ge(s_sp[i % 2], 16 * (i // 2))
                for kb in range(4):
                    n = 4 * i + kb
                    act.wait_ge(s_xt, n + 1)
                    nc.scalar.copy(xT[:, i % 2, 4 * kb:4 * kb + 4, 0:tok[i]],
                                   ps[:, 4 + kb, :].rearrange("p (k n) -> p k n", k=4)[:, :, 0:tok[i]]
                                   ).then_inc(s_xe, 1)
                    if n >= 1:
                        x_high(n - 1)
                if i == 0:
                    act.wait_ge(s_pool, 3)
                    act.wait_ge(s_cc, 2)
                else:
                    act.wait_ge(s_ssq, i)
                nc.scalar.activation(junk[0:tok[i], :], xN[0:tok[i], i % 2, :], ACT.Square,
                                     accum_out=stat[0:tok[i], 8 + i:9 + i]).then_inc(s_ssq, 1)
            x_high(19)
            act.wait_ge(s_ssq, 5)
            nc.scalar.activation(stat[:, 16:21], stat[:, 8:13], ACT.Sqrt, bias=stat[:, 0:1], scale=1.0 / D
                                 ).then_inc(s_rs, 1)
            for q in range(6):
                hi(Unit(-1, 2 + q), KIW if q < 2 else P)

            def hi4(p):
                for q in range(4):
                    hi(Unit(p, 4 + q))

            with act.Fori(0, 4) as i:
                hi4(P_QI + i)

            n = 0
            for i in range(1, 4):
                for hh in range(IH):
                    act.wait_ge(s_is, n + 1)
                    if n >= 2:
                        act.wait_ge(s_ia, n - 1)
                    nc.scalar.activation(rel[:, n % 2, 0:SW[i]], ps[:, 4 + n % 4, 0:SW[i]], ACT.Relu).then_inc(s_ir, 1)
                    n += 1
            act.wait_ge(s_nt, 1)
            act.wait_ge(s_xl, 20)
            act.wait_ge(s_proj, 9)
            rows_out(nc.scalar, kiN, ps[:, 4, 0:4 * ID], ps[0:NS, 5, 0:ID], ID, s_nc)
            act.wait_ge(s_ia, 3 * IH)
            for b in range(B):
                for g in range(2):
                    act.wait_ge(s_it, 2 * b + g + 1)
                    if b >= 2:
                        act.wait_ge(s_dt, 3 * (b - 1))
                    nc.scalar.copy(idxT[:, b % 2, 4 * g:4 * g + 4, :], ps[:, 5, :].rearrange("p (k n) -> p k n", k=4)
                                   ).then_inc(s_ic, 1)
                for c in range(3):
                    n = 3 * b + c
                    r, w = (P, 512) if c < 2 else (P // 2, NS)
                    act.wait_ge(s_dt, n + 1)
                    if n >= 2:
                        act.wait_ge(s_hs, n - 1)
                    nc.scalar.activation(rel[0:r, n % 2, 0:w], ps[0:r, 6 + n % 2, 0:w], ACT.Relu).then_inc(s_dr, 1)
            for c in range(CT):
                act.wait_ge(s_stt, c + 1)
                nc.scalar.copy(stT[:, c, :], ps[:, 4 + c % 4, 0:240]).then_inc(s_stc, 1)

            def sigmoid_gate(m):
                act.wait_ge(s_ev, m + 1)
                nc.scalar.activation(sg[:, :], sg[:, :], ACT.Sigmoid).then_inc(s_sg, 1)

            def state_rows(c):
                act.wait_ge(s_tt, c + 1)
                nc.scalar.copy(cout[:, bass.ds(c * P, P)], ps[0:CK - 1 + NS, 6, 0:P]).then_inc(s_co, 1)

            def tap_products(c, a0, a1):
                for k in range(a0, a1):
                    if k >= 3:
                        act.wait_ge(s_add, (NA - 1) * c + k - 2)
                    if k == 0:
                        dst = y2[:, :]
                    else:
                        dst = tap[:, (k - 1) % 2, :]
                    nc.scalar.activation(dst, gbuf[:, ND + k:ND + k + SEQ], ACT.Copy,
                                         scale=cw[:, bass.ds(c, 1), ND + k]).then_inc(s_tap, 1)

            def conv_highs(i):
                act.wait_ge(s_tg, i)
                if not (isinstance(i, int) and i == 1):
                    act.wait_ge(s_conv, CN * (i - 1))
                for q in range(4):
                    tap_products(i - 1, NA * q // 4, NA * (q + 1) // 4)
                    hi(Unit(P_U + i, 4 + q))

            def conv_step(i):
                conv_highs(i)
                sigmoid_gate(M_U + 2 * i + 1)
                state_rows(i - 1)

            hi4(P_U)
            sigmoid_gate(M_U + 1)
            conv_step(1)
            with act.Fori(2, CT) as i:
                conv_step(i)
            conv_highs(CT)
            state_rows(CT - 1)
            hi4(P_Q + 1)
            hi4(P_Q + 2)
            for c in range(CT):
                act.wait_ge(s_yc, c + 1)
                if c >= 2:
                    act.wait_ge(s_sqm, c - 1)
                nc.scalar.activation(sq[:, c % 2, :], y[:, c, :], ACT.Square).then_inc(s_sqd, 1)
            act.wait_ge(s_l2, 1)
            nc.scalar.activation(halves(rl[:, :]), ps[:, 4:6, 0:HALF], ACT.Sqrt, bias=stat[:, 0:1], scale=1.0 / CW_
                                 ).then_inc(s_sd, 1)
            hi4(P_Q + 3)
            for c in range(CT):
                act.wait_ge(s_yn, c + 1)
                nc.scalar.activation(y[:, c, :], y[:, c, :], ACT.Silu, bias=vec[:, 48 + c:49 + c],
                                     scale=vec[:, 40 + c:41 + c]).then_inc(s_ysl, 1)
            hi4(P_K)
            act.wait_ge(s_nt, 2)
            rows_out(nc.scalar, kN, flat[:, 2048:3072], ps[0:NS, 6, 0:256], 256, s_nc)
            act.wait_ge(s_ysl, CT)
            act.wait_ge(s_mm, 2 * M_OUT)
            for c in range(CT):
                nc.scalar.copy(xhi[:, 8 + c, :], y[:, c, :]).then_inc(s_yh, 1)
                if c == 1:
                    act.wait_ge(s_nt, 3)
                    rows_out(nc.scalar, vN, flat[:, 2048:3072], ps[0:NS, 6, 0:256], 256, s_nc)

            act.wait_ge(s_ko, 32)
            for x in range(32 + 3):
                if x < 32:
                    w = SW[x // 8]
                    act.wait_ge(s_nm, x + 1)
                    if x >= 3:
                        act.wait_ge(s_pt, x - 2)
                    nc.scalar.activation(pP[:, x % 3, 0:w], ps[:, (4, 5, 0, 1)[x % 4], 0:w], ACT.Exp,
                                         bias=stat[:, 24 + x % 4:25 + x % 4], scale=ASCALE,
                                         accum_out=stat[:, 28 + x % 4:29 + x % 4]).then_inc(s_p, 1)
                if 0 <= x - 2 < 32:
                    z = x - 2
                    act.wait_ge(s_pt, z + 1)
                    if z >= 2:
                        act.wait_ge(s_o, z - 1)
                    nb = z // 8 + 1
                    nc.scalar.copy(pPT[:, z % 2, 0:nb, :], ps[:, (6, 2)[z % 2], 0:P * nb].rearrange(
                        "p (k n) -> p k n", k=nb)).then_inc(s_pc, 1)
                if x >= 3 and (x - 3) % 4 == 3:
                    z = x - 3
                    act.wait_ge(s_o, z + 1)
                    h0, q0 = z % 8 - 3, P * (z // 8)
                    nc.scalar.copy(xhi[:, h0:h0 + 4, q0:q0 + P], ps[:, (7, 3)[z // 4 % 2], :].rearrange(
                        "p (k n) -> p k n", k=4)).then_inc(s_oh, 1)

            for g in range(2):
                for q in range(16 * g, 16 * g + 16):
                    act.wait_ge(s_chunk, 16 * g + q + 1)
                    if q >= 2:
                        act.wait_ge(s_ks, q - 1)
                    nc.scalar.copy(kpT[:, q % 2, 0, :], ps[:, 5, :]).then_inc(s_kca, 1)
                act.wait_ge(s_gm, g + 1)
                if g == 0:
                    act.wait_ge(s_o, 32)
                else:
                    act.wait_ge(s_gt, 5)
                nc.scalar.activation(pS[:, :], score_row, ACT.Exp, bias=stat[:, 32:33], scale=ASCALE,
                                     accum_out=stat[:, 33:34]).then_inc(s_gp, 1)
                for c in range(5):
                    act.wait_ge(s_gt, 5 * g + c + 1)
                    if g == 1 and c == 0:
                        act.wait_ge(s_gl, 2)
                    if c < 4:
                        nc.scalar.copy(pST[:, 4 * c:4 * c + 4, :], ps[:, 5 + c % 2, :].rearrange(
                            "p (k n) -> p k n", k=4)).then_inc(s_gc, 1)
                    else:
                        nc.scalar.copy(pST[0:NS, 16, :], ps[0:NS, 5, 0:P]).then_inc(s_gc, 1)
                if g == 1:
                    hi4(P_V)
                act.wait_ge(s_chunk, 32 * g + 32)
                nc.scalar.copy(oS[:, :], ps[:, 7, 0:256]).then_inc(s_os, 1)
                act.wait_ge(s_ot, g + 1)
                for kv in range(NKV):
                    nc.scalar.copy(mixed(xhi, kv, g), pv_bank(kv)).then_inc(s_gh, 1)

            def square(j):
                act.wait_ge(s_h, j + 1)
                act.wait_ge(s_sqs, j + 1)
                nc.scalar.activation(halves(sq2[:, :]), tile_of(h, j), ACT.Square).then_inc(s_sqh, 1)

            with act.Fori(0, 8) as i:
                for s in range(2):
                    hi(Unit(P_OUT + i, 4 + 2 * s))
                    hi(Unit(P_OUT + i, 5 + 2 * s))
                    square(2 * i + s)
            act.wait_ge(s_mm, 2 * M_FFN)
            for k in range(KT):
                nc.scalar.copy(xhi[:, k, :], hg[:, k, :]).then_inc(s_n2h, 1)
            act.wait_ge(s_r2, 1)
            nc.scalar.activation(halves(rstd2[:, :]), ps[:, 4:6, 0:HALF], ACT.Sqrt, bias=stat[:, 0:1], scale=1.0 / D
                                 ).then_inc(s_r2s, 1)

            def ffn_act(c, last):
                p0 = P_FFN + P_CH * c
                with act.Fori(0, CJ) as j:
                    hi(Unit(p0 + j, 4))
                    hi(Unit(p0 + j, 5))
                    act.wait_ge(s_ev, 2 * p0 + 2 * j + 2)
                    nc.scalar.activation(gt[:, :], gt[:, :], ACT.Silu).then_inc(s_silu, 1)
                    hi(Unit(p0 + j, 6))
                    hi(Unit(p0 + j, 7))
                    act.wait_ge(s_hm, CJ * c + j + 1)
                    nc.scalar.copy(tile_of(hidh, j), halves(ut[:, :])).then_inc(s_hh, 1)
                with act.Fori(0, 7 if last else 8) as i:
                    hi4(p0 + CJ + i)

            with act.Fori(0, CH - 1) as c:
                ffn_act(c, False)
            ffn_act(CH - 1, True)

            for i in range(5):
                act.wait_ge(s_yt, 4 * (i + 1))
                if i == 0:
                    act.wait_ge(s_mm, 2 * M_ALL)
                nc.scalar.activation(junk2[0:tok[i], :], row_banks(i), ACT.Square,
                                     accum_out=stat[0:tok[i], 40 + i:41 + i]).then_inc(s_ys, 1)
                act.wait_ge(s_ys, 2 * i + 1)
                nc.scalar.activation(stat[0:tok[i], 48 + i:49 + i], stat[0:tok[i], 40 + i:41 + i], ACT.Sqrt,
                                     bias=stat[0:tok[i], 0:1], scale=1.0 / D).then_inc(s_ys, 1)

        @block.vector
        def _(dve):
            ve = nc.vector
            ch = Chain(dve, s_dve)

            def lo(u, cols=P):
                dve.wait_ge(s_hi, u.n + 1)
                ve.tensor_tensor(wlo[:, u.slot, :, 0:cols], raw[:, u.slot, :, 0:cols],
                                 whi[:, u.slot, :, 0:cols].bitcast(F32), ALU.subtract).then_inc(s_lo, 1)

            def x_low(n):
                i, kb = divmod(n, 4)
                dve.wait_ge(s_xh, n + 1)
                dst = (slice(None), slice(4 * kb, 4 * kb + 4), slice(P * i, P * i + tok[i]))
                ve.tensor_tensor(xlo[dst], xg[:, n % 2, :, 0:tok[i]], xhi[dst].bitcast(F32), ALU.subtract
                                 ).then_inc(s_xl, 1)

            dve.wait_ge(s_cc, 2)
            for n in range(20):
                i, kb = divmod(n, 4)
                dve.wait_ge(s_xe, n + 1)
                if n >= 2:
                    dve.wait_ge(s_xl, n - 1)
                ve.tensor_tensor(xg[:, n % 2, :, 0:tok[i]], xT[:, i % 2, 4 * kb:4 * kb + 4, 0:tok[i]],
                                 vec[:, 4 * kb:4 * kb + 4].unsqueeze(2).to_broadcast([P, 4, tok[i]]), ALU.mult
                                 ).then_inc(s_xg, 1)
                if n >= 1:
                    x_low(n - 1)
            x_low(19)
            dve.wait_ge(s_vec, 16 * 7)
            dve.wait_ge(s_const, 16 * 3)
            ve.tensor_copy(identb[:, :], ident[:, :])
            ve.tensor_copy(rowsel[:, :, :], rowselF[:, :, :])
            ve.tensor_copy(biasP[:, 0:P], causF[:, :]).then_inc(s_caus, 1)
            for q in range(4):
                lo(Unit(-1, 2 + q), KIW if q < 2 else P)
            dve.wait_ge(s_rs, 1)
            ch.link(ve.reciprocal(stat[:, 16:21], stat[:, 16:21]))
            for i in range(5):
                ve.tensor_scalar(diag[0:tok[i], i, 0:tok[i]], ident[0:tok[i], 0:tok[i]], stat[0:tok[i], 16 + i:17 + i],
                                 None, ALU.mult).then_inc(s_rd, 1)
            lo(Unit(-1, 6))
            lo(Unit(-1, 7))
            dve.wait_ge(s_rb, 1)
            ve.tensor_copy(rstd1[:, 0:SEQ], ps[:, 4, :])
            ch.link(ve.tensor_copy(rstd1[:, SEQ:NT], ps[:, 5, 0:NS]))
            ch.link(ve.tensor_tensor(tab[:, :, :], tab[:, :, :], rstd1[:, :].unsqueeze(1).to_broadcast([P, 4, NT]),
                                     ALU.mult))
            rs2 = halves(rstd1[:, :])
            c1, s1, c2, s2 = (halves(tab[:, n, :]) for n in range(4))
            rt2 = halves(rt[:, :])

            dve.wait_ge(s_mm, 2)
            ki2 = halves(kiT[:, :])
            ve.tensor_tensor(ki2[0:64], acc(1, 0, 64), c2[0:64], ALU.mult)
            ve.tensor_tensor(rt2[0:32], acc(1, 32, 64), s2[0:32], ALU.mult)
            ve.tensor_tensor(rt2[32:64], acc(1, 0, 32), s2[32:64], ALU.mult)
            ve.tensor_tensor(halves(wT[:, :]), acc(1, 64, 80), rs2[0:16], ALU.mult).then_inc(s_ev, 1)
            dve.wait_ge(s_ev, 1)
            ch.link(ve.tensor_tensor(kiT[0:64, :], kiT[0:64, :], rt[0:64, :], ALU.add))
            ve.tensor_copy(kiT[64:128, :], kiT[0:64, :]).then_inc(s_proj, 1)

            def rope(dst, slot, m, before, cos, sin, width):
                dve.wait_ge(s_proj, before)
                ve.tensor_tensor(dst, acc(slot), cos, ALU.mult)
                r = width // 2
                for p0 in range(0, P, r):
                    q0 = p0 + r if p0 // r % 2 == 0 else p0 - r
                    ins = ve.tensor_tensor(rt2[p0:p0 + r], acc(slot, q0, q0 + r), sin[p0:p0 + r], ALU.mult)
                ins.then_inc(s_ev, 1)
                dve.wait_ge(s_ev, m + 1)
                ve.tensor_tensor(dst, dst, rt2, ALU.add).then_inc(s_proj, 1)

            def pair(p, first, second, mid=None, lows=True):
                if lows:
                    lo(Unit(p, 4))
                    lo(Unit(p, 5))
                dve.wait_ge(s_mm, 4 * p + 4)
                first()
                if mid:
                    mid()
                if lows:
                    lo(Unit(p, 6))
                    lo(Unit(p, 7))
                dve.wait_ge(s_mm, 4 * p + 6)
                second()

            def rope_pair(p, dst, j, before, cos, sin, width, **more):
                pair(p, lambda: rope(tile_of(dst, j), 0, 2 * p + 1, before, cos, sin, width),
                     lambda: rope(tile_of(dst, j + 1), 1, 2 * p + 2, before + 1, cos, sin, width), **more)

            dve.wait_ge(s_sp[0], 48)
            dve.wait_ge(s_sp[1], 32)
            with dve.Fori(0, 4) as i:
                rope_pair(P_QI + i, qT, 2 * i, 1 + 2 * i, c2, s2, ID)

            dve.wait_ge(s_wt, 1)
            ve.tensor_scalar(wiP[:, :, :], ps[:, 7, 0:64].rearrange("p (i h) -> p i h", i=4), ISCALE, None, ALU.mult
                             ).then_inc(s_wtc, 1)
            dve.wait_ge(s_wtc, 1)
            n = 0
            for i in range(1, 4):
                for hh in range(IH):
                    dve.wait_ge(s_ir, n + 1)
                    dst = scP[:, SO[i]:SO[i] + SW[i]]
                    if hh == 0:
                        ve.tensor_scalar(dst, rel[:, n % 2, 0:SW[i]], wiP[:, i, 0:1], None, ALU.mult).then_inc(s_ia, 1)
                    else:
                        dve.wait_ge(s_ia, n)
                        ve.scalar_tensor_tensor(dst, rel[:, n % 2, 0:SW[i]], wiP[:, i, hh:hh + 1], dst,
                                                ALU.mult, ALU.add).then_inc(s_ia, 1)
                    n += 1
            dve.wait_ge(s_proj, 9)
            ve.memset(wsel[:, :, :, :], 0.0)
            ch.link(ve.memset(qiS[:, :, :, :, :], 0.0))
            for half in range(2):
                for src in range(2):
                    ve.tensor_copy(qiS[64 * half:64 * half + 64, :, half, src::2, :].rearrange("p b j t -> p j b t"),
                                   qT[64 * src:64 * src + 64, :, SEQ:NT].rearrange("p j (b t) -> p j b t", t=T))
            dve.wait_ge(s_wt, 2)
            dve.wait_ge(s_const, 16 * NCONST)
            for par in range(2):
                r = slice(64 * par, 64 * par + 64)
                for b in range(B):
                    last = ve.scalar_tensor_tensor(wsel[r, b, par, T * b:T * b + T], ps[r, 7, T * b:T * b + T],
                                                   ISCALE, tsel[r, T * b:T * b + T], ALU.mult, ALU.mult)
            last.then_inc(s_wtc, 1)

            def topk_waits(count):
                dve.wait_ge(s_topk, count)
                ve.tensor_copy(stat[:, 61:62], stat[:, 60:61])

            dve.wait_ge(s_pool, 6)
            with dve.Fori(0, KP_ // 8) as r:
                for i in range(1, 4):
                    ve.max(m8[:, i, :], scP[:, SO[i]:SO[i] + SW[i]]).then_inc(s_topk, 1)
                topk_waits(6 * r + 3)
                for i in range(1, 4):
                    v = scP[:, SO[i]:SO[i] + SW[i]]
                    ve.match_replace(v, m8[:, i, :], v, TAKEN).then_inc(s_topk, 1)
                topk_waits(6 * r + 6)
            for i in range(1, 4):
                last = ve.tensor_scalar(biasP[:, BO[i]:BO[i] + SW[i]], scP[:, SO[i]:SO[i] + SW[i]],
                                        0.5 * (INVALID + TAKEN), MASKED, ALU.is_gt, ALU.mult)
            last.then_inc(s_bias, 1)

            dve.wait_ge(s_hs, 3 * B)
            for par in range(2):
                for hf in range(2):
                    dst = scS[:, 0:PAST].rearrange("p (k r n) -> p k r n", r=2, n=P)[:, 4 * hf:4 * hf + 4, par, :]
                    ve.tensor_copy(dst, ps[NS * par:NS * par + NS, hf, :].rearrange("p (k n) -> p k n", k=4))
            ch.link(ve.tensor_tensor(scS[:, PAST:NSK], ps[0:NS, 4, 0:NS], tailm[:, :], ALU.add))
            ve.memset(gbuf[:, 0:CK - 1], 0.0).then_inc(s_xs, 1)

            def taps(c, k0, k1):
                yp = y[:, bass.ds(c, 1), 0:SEQ].rearrange("p a n -> p (a n)")
                for k in range(k0, k1):
                    wk = cw[:, bass.ds(c, 1), k]
                    if k == 0:
                        ve.tensor_scalar(yp, gbuf[:, 0:SEQ], wk, vec[:, bass.ds(32 + c, 1)], ALU.mult, ALU.add
                                         ).then_inc(s_conv, 1)
                    elif k == 1:
                        ve.tensor_scalar(y3[:, :], gbuf[:, 1:1 + SEQ], wk, None, ALU.mult).then_inc(s_conv, 1)
                    else:
                        dst = y3[:, :] if k % 2 else yp
                        dve.wait_ge(s_conv, CN * c + k - 1)
                        ve.scalar_tensor_tensor(dst, gbuf[:, k:k + SEQ], wk, dst, ALU.mult, ALU.add
                                                ).then_inc(s_conv, 1)

            def convolved(c):
                taps(c, ND // 2, ND)
                ys = y[:, bass.ds(c, 1), SEQ:NT].rearrange("p a n -> p (a n)")
                dve.wait_ge(s_smul, T * c + T)
                ve.reduce_sum(ys, tapS[:, :, :, :].rearrange("p b t k -> p (b t) k"), AX.X).then_inc(s_ssum, 1)
                dve.wait_ge(s_ssum, 2 * c + 1)
                ve.tensor_scalar(ys, ys, vec[:, bass.ds(32 + c, 1)], None, ALU.add).then_inc(s_ssum, 1)
                yp = y[:, bass.ds(c, 1), 0:SEQ].rearrange("p a n -> p (a n)")
                dve.wait_ge(s_conv, CN * c + ND)
                ve.tensor_tensor(yp, yp, y3[:, :], ALU.add).then_inc(s_conv, 1)
                dve.wait_ge(s_conv, CN * c + ND + 1)
                dve.wait_ge(s_add, (NA - 1) * c + NA - 1)
                ve.tensor_tensor(yp, yp, y2[:, :], ALU.add).then_inc(s_conv, 1)

            def gated(c):
                if not (isinstance(c, int) and c == 0):
                    dve.wait_ge(s_conv, CN * c)
                ve.tensor_copy(gs[:, :, 0:CK - 1], stT[:, bass.ds(c, 1), :].rearrange("p a (b s) -> p (a b) s", b=B))
                dve.wait_ge(s_sg, c + 1)
                ve.tensor_tensor(gbuf[:, CK - 1:CK - 1 + SEQ], ga[:, 0:SEQ], sg[:, 0:SEQ], ALU.mult)
                ch.link(ve.tensor_tensor(gs[:, :, CK - 1:], ga[:, SEQ:].rearrange("p (b t) -> p b t", b=B),
                                         sg[:, SEQ:].rearrange("p (b t) -> p b t", b=B), ALU.mult))
                if not (isinstance(c, int) and c == 0):
                    dve.wait_ge(s_tt, c)
                ve.tensor_copy(tg[:, 0:CK - 1], gbuf[:, SEQ:SEQ + CK - 1])
                ve.tensor_copy(tg[:, CK - 1:CK - 1 + NS].rearrange("p (b t) -> p b t", b=B), gs[:, :, CK - 1:]).then_inc(s_tg, 1)

            def plain(dst, slot):
                ve.tensor_tensor(dst, acc(slot), rs2, ALU.mult).then_inc(s_ev, 1)

            def topk_sample(rounds, base):
                with dve.Fori(0, rounds) as r:
                    topk_round(base + 2 * r)

            def topk_round(base):
                half_round(base, 0)
                half_round(base, 1)

            def half_round(base, n):
                if n % 2 == 0:
                    ve.max(m8[0:NS, 0, :], scS[:, :]).then_inc(s_topk, 1)
                else:
                    ve.match_replace(scS[:, :], m8[0:NS, 0, :], scS[:, :], TAKEN).then_inc(s_topk, 1)
                topk_waits(base + n + 1)

            def u_step(c, conv):
                pair(P_U + c, lambda: plain(halves(ga[:, :]), 0), lambda: plain(halves(sg[:, :]), 1),
                     mid=(lambda: taps(c - 1, 0, ND // 2)) if conv else None, lows=False)
                if conv:
                    convolved(c - 1)
                gated(c)
                topk_round(T0 + 2 * c)

            dve.wait_ge(s_stc, CT)
            dve.wait_ge(s_kio, 32)
            ch.link(ve.memset(tg[:, :], 0.0))
            T0 = 6 * (KP_ // 8)
            u_step(0, False)
            topk_sample(EARLY, T0 + 2)
            T0 += 2 * EARLY
            with ch.loop(1, CT, 1) as c:
                u_step(c, True)
            T0 += 2 * CT
            dve.wait_ge(s_tg, CT)
            rope_pair(P_Q, qT, 0, 9, c1, s1, HD, mid=lambda: taps(CT - 1, 0, ND // 2), lows=False)
            convolved(CT - 1)
            topk_sample(4, T0)
            T0 += 8
            rope_pair(P_Q + 1, qT, 2, 11, c1, s1, HD, lows=False)
            topk_sample(2, T0)
            T0 += 4
            dve.wait_ge(s_l1, 1)
            ve.tensor_scalar(halves(mu[:, :]), ps[:, 6:8, 0:HALF], 1.0 / CW_, None, ALU.mult).then_inc(s_mu, 1)
            topk_sample(2, T0)
            T0 += 4
            rope_pair(P_Q + 2, qT, 4, 13, c1, s1, HD, lows=False)
            topk_sample(3, T0)
            T0 += 6
            dve.wait_ge(s_sd, 1)
            ve.reciprocal(rl[:, :], rl[:, :]).then_inc(s_rl, 1)
            rope_pair(P_Q + 3, qT, 6, 15, c1, s1, HD, lows=False)
            topk_sample(3, T0)
            T0 += 6
            rope_pair(P_K, kT, 0, 17, c1, s1, HD, lows=False)
            topk_sample(3, T0)
            T0 += 6
            pair(P_V, lambda: plain(tile_of(vT, 0), 0), lambda: plain(tile_of(vT, 1), 1), lows=False)
            for c in range(CT):
                dve.wait_ge(s_yh, c + 1)
                ve.tensor_tensor(xlo[:, 8 + c, :], y[:, c, :], xhi[:, 8 + c, :].bitcast(F32), ALU.subtract
                                 ).then_inc(s_mix, 1)
            for kv in range(NKV):
                last = ve.tensor_copy(
                    qpad[:, :, kv, 16 * kv:16 * kv + 16].rearrange("p b (g t) -> p g b t", g=GRP),
                    qT[:, GRP * kv:GRP * kv + GRP, SEQ:NT].rearrange("p g (b t) -> p g b t", b=B))
            last.then_inc(s_qp, 1)


            for x in range(32 + 4):
                if x < 32:
                    w = SW[x // 8]
                    dve.wait_ge(s_s, x + 1)
                    if x >= 4:
                        dve.wait_ge(s_p, x - 3)
                    ve.reduce_max(stat[:, 36 + x % 4:37 + x % 4], ps[:, (4, 5, 0, 1)[x % 4], 0:w], AX.X
                                  ).then_inc(s_nm2, 1)
                    dve.wait_ge(s_nm2, x + 1)
                    ve.tensor_scalar(stat[:, 24 + x % 4:25 + x % 4], stat[:, 36 + x % 4:37 + x % 4], -ASCALE, None,
                                     ALU.mult).then_inc(s_nm, 1)
                if 0 <= x - 1 < 32:
                    z = x - 1
                    dve.wait_ge(s_p, z + 1)
                    ch.link(ve.reciprocal(stat[:, 28 + z % 4:29 + z % 4], stat[:, 28 + z % 4:29 + z % 4]))
                    ve.tensor_scalar(pP[:, z % 3, 0:SW[z // 8]], pP[:, z % 3, 0:SW[z // 8]],
                                     stat[:, 28 + z % 4:29 + z % 4], None, ALU.mult).then_inc(s_pn, 1)
                if x < 32 and x % 4 == 1:
                    half_round(T0, x // 4)
                if x >= 4 and (x - 4) % 4 == 3:
                    z = x - 4
                    dve.wait_ge(s_oh, z // 4 + 1)
                    h0, q0 = z % 8 - 3, P * (z // 8)
                    ve.tensor_tensor(xlo[:, h0:h0 + 4, q0:q0 + P],
                                     ps[:, (7, 3)[z // 4 % 2], :].rearrange("p (k n) -> p k n", k=4),
                                     xhi[:, h0:h0 + 4, q0:q0 + P].bitcast(F32), ALU.subtract).then_inc(s_ol, 1)

            assert T0 + LATE == 6 * (KP_ // 8) + 2 * (KS_ // 8)
            dve.wait_ge(s_cvo, 48)
            ve.tensor_scalar(biasS[:, :], scS[:, :], 0.5 * (INVALID + TAKEN), MASKED, ALU.is_gt, ALU.mult
                             ).then_inc(s_bias, 1)

            for g in range(2):
                for q in range(16 * g, 16 * g + 16):
                    dve.wait_ge(s_chunk, 16 * g + q + 1)
                    if q >= 2:
                        dve.wait_ge(s_ks, q - 1)
                    ve.tensor_copy(kpT[:, q % 2, 1, :], ps[:, 6, :]).then_inc(s_kcd, 1)
                dve.wait_ge(s_gb, g + 1)
                ch.link(ve.reduce_max(stat[:, 34:35], score_row, AX.X))
                ve.tensor_scalar(stat[:, 32:33], stat[:, 34:35], -ASCALE, None, ALU.mult).then_inc(s_gm, 1)
                dve.wait_ge(s_gp, g + 1)
                ch.link(ve.reciprocal(stat[:, 33:34], stat[:, 33:34]))
                ve.tensor_scalar(pS[:, :], pS[:, :], stat[:, 33:34], None, ALU.mult).then_inc(s_gn, 1)
                if g == 1:
                    dve.wait_ge(s_lo, 4 * P_V + 6)
                    for q in range(4):
                        lo(Unit(P_V, 4 + q))
                for kv in range(NKV):
                    dve.wait_ge(s_gh, 2 * g + kv + 1)
                    ve.tensor_tensor(mixed(xlo, kv, g), pv_bank(kv), mixed(xhi, kv, g).bitcast(F32),
                                     ALU.subtract).then_inc(s_gl, 1)

            ve.memset(sqa[:, :], 0.0).then_inc(s_sqs, 1)
            dve.wait_ge(s_sqs, 1)

            def residual(j, s, count):
                dve.wait_ge(s_xr[s], count)
                ve.tensor_tensor(tile_of(h, j), acc(s), halves(xTr[:, s, :]), ALU.add).then_inc(s_ev, 1)
                dve.wait_ge(s_ev, M_OUT + j + 1)
                ve.tensor_scalar(tile_of(hg, j), tile_of(h, j), vec[:, bass.ds(16 + j, 1)], None, ALU.mult
                                 ).then_inc(s_h, 1)
                dve.wait_ge(s_sqh, j + 1)
                ve.tensor_tensor(sqa[:, :], sqa[:, :], sq2[:, :], ALU.add).then_inc(s_sqs, 1)
                dve.wait_ge(s_sqs, j + 2)

            with dve.Fori(0, 8) as i:
                pair(P_OUT + i, lambda: residual(2 * i, 0, 16 * i + 16), lambda: residual(2 * i + 1, 1, 16 * i + 16))
            for k in range(KT):
                dve.wait_ge(s_n2h, k + 1)
                ve.tensor_tensor(xlo[:, k, :], hg[:, k, :], xhi[:, k, :].bitcast(F32), ALU.subtract).then_inc(s_n2, 1)
            dve.wait_ge(s_r2s, 1)
            ch.link(ve.reciprocal(rstd2[:, :], rstd2[:, :]))

            r22 = halves(rstd2[:, :])

            def ffn_dve(c, last):
                p0 = P_FFN + P_CH * c

                def up(j):
                    ve.tensor_tensor(halves(ut[:, :]), acc(1), r22, ALU.mult).then_inc(s_ev, 1)
                    dve.wait_ge(s_ev, 2 * (p0 + j) + 3)
                    dve.wait_ge(s_silu, CJ * c + j + 1)
                    ve.tensor_tensor(ut[:, :], ut[:, :], gt[:, :], ALU.mult).then_inc(s_hm, 1)
                    dve.wait_ge(s_hh, CJ * c + j + 1)
                    ve.tensor_tensor(tile_of(hidl, j), halves(ut[:, :]), tile_of(hidh, j).bitcast(F32), ALU.subtract
                                     ).then_inc(s_hid, 1)
                    dve.wait_ge(s_hid, CJ * c + j + 1)

                with dve.Fori(0, CJ) as j:
                    pair(p0 + j,
                         lambda: ve.tensor_tensor(halves(gt[:, :]), acc(0), r22, ALU.mult).then_inc(s_ev, 1),
                         lambda: up(j))

                def add(j, s):
                    ve.tensor_tensor(tile_of(h, j), acc(s), tile_of(h, j), ALU.add).then_inc(s_ev, 1)

                with dve.Fori(0, 7 if last else 8) as i:
                    pair(p0 + CJ + i, lambda: add(2 * i, 0), lambda: add(2 * i + 1, 1))
                if last:
                    for s in range(2):
                        dve.wait_ge(s_mm, 2 * M_ALL - 2 + 2 * s)
                        add(14 + s, s)

            with dve.Fori(0, CH - 1) as c:
                ffn_dve(c, False)
            ffn_dve(CH - 1, True)

            dve.wait_ge(s_gf, 16)
            for i in range(5):
                dve.wait_ge(s_ys, 2 * i + 2)
                if i >= 2:
                    dve.wait_ge(s_yo[i % 2], 16 * (i // 2))
                ch.link(ve.reciprocal(stat[0:tok[i], 48 + i:49 + i], stat[0:tok[i], 48 + i:49 + i]))
                ve.scalar_tensor_tensor(yo[0:tok[i], i % 2, :], row_banks(i), stat[0:tok[i], 48 + i:49 + i],
                                        gfb[0:tok[i], :], ALU.mult, ALU.mult).then_inc(s_yd, 1)

        @block.tensor
        def _(pe):
            te = nc.tensor

            def unit(u, slot, hf, k=UK, k0=0, cols=P, xh=xhi, xl=xlo, as_ready=None):
                pe.wait_ge(s_lo, u.n + 1)
                for t in range(k):
                    if as_ready is not None:
                        pe.wait_ge(as_ready, k0 + t + 1)
                    for w, x in ((whi, xh), (whi, xl), (wlo, xh)):
                        for half in range(2):
                            ins = te.matmul(ps[0:cols, 2 * slot + half, 0:HALF], w[:, u.slot, t, 0:cols],
                                            x[:, k0 + t, HALF * half:HALF * half + HALF],
                                            start=(hf == 0 and t == 0 and w is whi and x is xh),
                                            stop=(hf == 1 and t == k - 1 and w is wlo))
                ins.then_inc(s_mm, 1)

            def tile(p, s, as_ready=None):
                if not (isinstance(p, int) and p == 0 and s == 0):
                    pe.wait_ge(s_ev, 2 * p + s)
                for hf in range(2):
                    unit(Unit(p, 2 * s + hf), s, hf, k0=UK * hf, as_ready=as_ready)

            def pair(p):
                tile(p, 0)
                tile(p, 1)

            pe.wait_ge(s_vec, 16 * 7)
            te.transpose(ps[:, 0, 0:56], vecN[:, :], ident[0:56, 0:56])
            for c in range(CT):
                ins = te.transpose(ps[:, 1, CK * c:CK * c + CK], cwN[:, P * c:P * c + P], ident[0:CK, 0:CK])
            ins.then_inc(s_ct, 1)
            for i in range(5):
                r = tok[i]
                pe.wait_ge(s_xn[i % 2], 16 * (i // 2 + 1))
                for kb in range(4):
                    if i >= 1:
                        pe.wait_ge(s_xe, 4 * (i - 1) + kb + 1)
                    for k in range(4):
                        ins = te.transpose(ps[:, 4 + kb, P * k:P * k + r],
                                           xN[0:r, i % 2, P * (4 * kb + k):P * (4 * kb + k) + P], ident[0:r, 0:r])
                    ins.then_inc(s_xt, 1)
            pe.wait_ge(s_xl, 20)
            pe.wait_ge(s_cc, 2)
            for hf in range(2):
                unit(Unit(-1, 2 + hf), 1, hf, k0=UK * hf, cols=KIW)
            pe.wait_ge(s_pool, 1)
            pe.wait_ge(s_rd, 5)
            pe.wait_ge(s_xe, 20)
            for i in range(4):
                te.matmul(ps[:, 4, P * i:P * i + P], ones[:, :], diag[:, i, :], start=True, stop=True)
            te.matmul(ps[:, 5, 0:NS], ones[0:NS, :], diag[0:NS, 4, 0:NS], start=True, stop=True).then_inc(s_rb, 1)
            with pe.Fori(0, 4) as i:
                pair(P_QI + i)

            pe.wait_ge(s_proj, 1)
            for i in range(4):
                ins = te.transpose(ps[:, 7, IH * i:IH * i + IH], wT[:, P * i:P * i + P], ident[0:IH, 0:IH])
            ins.then_inc(s_wt, 1)
            pe.wait_ge(s_proj, 9)
            pe.wait_ge(s_wtc, 1)
            n = 0
            for i in range(1, 4):
                for hh in range(IH):
                    if n >= 4:
                        pe.wait_ge(s_ir, n - 3)
                    p0 = 64 * (hh % 2)
                    te.matmul(ps[:, 4 + n % 4, 0:SW[i]], qT[p0:p0 + 64, hh // 2, P * i:P * i + P],
                              kiT[p0:p0 + 64, 0:SW[i]], start=True, stop=True).then_inc(s_is, 1)
                    n += 1
            pe.wait_ge(s_ir, 3 * IH)
            for i in range(4):
                te.transpose(ps[:, 4, ID * i:ID * i + ID], kiT[0:64, P * i:P * i + P], ident[0:64, 0:64])
            te.transpose(ps[0:NS, 5, 0:ID], kiT[0:64, SEQ:NT], ident[0:64, 0:64]).then_inc(s_nt, 1)
            pe.wait_ge(s_const, 16 * NCONST)
            te.matmul(ps[:, 7, 0:NS], hsel[:, :], wT[:, SEQ:NT], start=True, stop=True).then_inc(s_wt, 1)
            pe.wait_ge(s_nc, 1)
            pe.wait_ge(s_ev, M_U)
            pe.wait_ge(s_wtc, 2)

            def head_sum(n):
                b, c = divmod(n, 3)
                pe.wait_ge(s_dr, n + 1)
                if c < 2:
                    te.matmul(ps[0:2 * NS, c, :], wsel[:, b, :, :].rearrange("p r n -> p (r n)"), rel[:, n % 2, :],
                              start=(b == 0), stop=(b == B - 1)).then_inc(s_hs, 1)
                else:
                    te.matmul(ps[0:NS, 4, 0:NS], wsel[0:64, b, 0, :], rel[0:64, n % 2, 0:NS],
                              start=(b == 0), stop=(b == B - 1)).then_inc(s_hs, 1)

            for b in range(B):
                pe.wait_ge(s_ik[b % IB], 16 * (NPG if b < IB else NPG + NPG // 2))
                if b >= IB:
                    pe.wait_ge(s_iks[b % IB], 16 * (NPG // 2))
                for g in range(2):
                    if b or g:
                        pe.wait_ge(s_ic, 2 * b + g)
                    for k in range(4):
                        q = 8 * g + 2 * k
                        ins = te.transpose(ps[:, 5, P * k:P * k + P],
                                           idxN[:, b % IB, q:q + 2, :].rearrange("p a d -> p (a d)"), ident[:, :])
                    ins.then_inc(s_it, 1)
                pe.wait_ge(s_ic, 2 * b + 2)
                for c in range(3):
                    n = 3 * b + c
                    if n >= 2:
                        pe.wait_ge(s_dr, n - 1)
                    if c < 2:
                        te.matmul(ps[:, 6 + n % 2, :], qiS[:, b, :, :, :].rearrange("p r h t -> p (r h t)"),
                                  idxT[:, b % 2, 4 * c:4 * c + 4, :].rearrange("p k n -> p (k n)"),
                                  start=True, stop=True).then_inc(s_dt, 1)
                    else:
                        te.matmul(ps[0:64, 6 + n % 2, 0:NS], qiS[0:64, b, 0, :, :].rearrange("p h t -> p (h t)"),
                                  kiT[0:64, SEQ:NT], start=True, stop=True).then_inc(s_dt, 1)
                    if n >= 1:
                        head_sum(n - 1)
            head_sum(3 * B - 1)
            pe.wait_ge(s_st, 16)
            pe.wait_ge(s_xs, 1)
            for c in range(CT):
                if c >= 4:
                    pe.wait_ge(s_stc, c - 3)
                for half in range(2):
                    ins = te.transpose(ps[:, 4 + c % 4, 120 * half:120 * half + 120], stN[:, half, P * c:P * c + P],
                                       ident[0:120, 0:120])
                ins.then_inc(s_stt, 1)
            pe.wait_ge(s_stc, CT)

            def new_state(c):
                pe.wait_ge(s_tg, c + 1)
                if not (isinstance(c, int) and c == 0):
                    pe.wait_ge(s_co, c)
                te.transpose(ps[:, 6, 0:P], tg[:, :], ident[:, :]).then_inc(s_tt, 1)

            pair(P_U)
            with pe.Fori(1, CT) as i:
                tile(P_U + i, 0)
                new_state(i - 1)
                tile(P_U + i, 1)
            tile(P_Q, 0)
            new_state(CT - 1)
            tile(P_Q, 1)
            pair(P_Q + 1)
            pe.wait_ge(s_conv, CN * CT)
            pe.wait_ge(s_ssum, 2 * CT)
            pe.wait_ge(s_co, CT)
            for half in range(2):
                for c in range(CT):
                    ins = te.matmul(ps[:, 6 + half, 0:HALF], ones[:, :], y[:, c, HALF * half:HALF * half + HALF],
                                    start=(c == 0), stop=(c == CT - 1))
            ins.then_inc(s_l1, 1)
            pair(P_Q + 2)
            for c in range(CT):
                pe.wait_ge(s_sqd, c + 1)
                for half in range(2):
                    ins = te.matmul(ps[:, 4 + half, 0:HALF], ones[:, :], sq[:, c % 2, HALF * half:HALF * half + HALF],
                                    start=(c == 0), stop=(c == CT - 1))
                ins.then_inc(s_sqm, 1) if c < CT - 1 else ins.then_inc(s_l2, 1)
            pair(P_Q + 3)
            pair(P_K)

            def in_rows(src):
                for i in range(5):
                    for kv in range(NKV):
                        r = tok[i]
                        ins = te.transpose(ps[0:r, 4 + i // 2, 256 * (i % 2) + P * kv:256 * (i % 2) + P * kv + P],
                                           src[:, kv, P * i:P * i + r], ident[:, :])
                ins.then_inc(s_nt, 1)

            tile(P_V, 0)
            pe.wait_ge(s_proj, 1 + 8 + 8 + 2)
            pe.wait_ge(s_sd, 1)
            in_rows(kT)
            tile(P_V, 1)
            pe.wait_ge(s_ev, M_OUT)
            pe.wait_ge(s_nc, 2)
            in_rows(vT)

            pe.wait_ge(s_bias, 1)
            pe.wait_ge(s_nc, 3)
            for x in range(32 + 3):
                if x < 32:
                    i, hh = divmod(x, 8)
                    w = SW[i]
                    bank = (4, 5, 0, 1)[x % 4]
                    if x >= 4:
                        pe.wait_ge(s_p, x - 3)
                    te.matmul(ps[:, bank, 0:w], identb[:, :], biasP[:, BO[i]:BO[i] + w], start=True, stop=False)
                    te.matmul(ps[:, bank, 0:w], qT[:, hh, P * i:P * i + P], kT[:, hh // GRP, 0:w],
                              start=False, stop=True).then_inc(s_s, 1)
                if 0 <= x - 2 < 32:
                    z = x - 2
                    pe.wait_ge(s_pn, z + 1)
                    if z >= 2:
                        pe.wait_ge(s_pc, z - 1)
                    for k in range(z // 8 + 1):
                        ins = te.transpose(ps[:, (6, 2)[z % 2], P * k:P * k + P], pP[:, z % 3, P * k:P * k + P],
                                           ident[:, :])
                    ins.then_inc(s_pt, 1)
                if x >= 3:
                    z = x - 3
                    i, hh = divmod(z, 8)
                    pe.wait_ge(s_pc, z + 1)
                    if z % 4 == 0 and z >= 8:
                        pe.wait_ge(s_ol, z // 4 - 1)
                    for k in range(i + 1):
                        ins = te.matmul(ps[:, (7, 3)[z // 4 % 2], P * (z % 4):P * (z % 4) + P],
                                        vN[:, k, P * (hh // GRP):P * (hh // GRP) + P], pPT[:, z % 2, k, :],
                                        start=(k == 0), stop=(k == i))
                    ins.then_inc(s_o, 1)

            pe.wait_ge(s_bias, 2)
            pe.wait_ge(s_qp, 1)
            pe.wait_ge(s_ol, 8)

            def keys(q):
                n = 32 * (q // 16) + q % 16
                pe.wait_ge(s_pg[n % SLOTS], 16 * SPP * (n // SLOTS + 1))
                pe.wait_ge(s_pgp[n % SLOTS], 16 * (4 - SPP) * (n // SLOTS + 1))
                if q >= 1:
                    pe.wait_ge(s_kca, q)
                    pe.wait_ge(s_kcd, q)
                for kv in range(NKV):
                    for k in range(4):
                        ins = te.transpose(ps[:, 5 + kv, P * k:P * k + P], page_slot(n)[:, k, P * kv:P * kv + P],
                                           ident[:, :])
                ins.then_inc(s_chunk, 1)

            for g in range(2):
                if g == 1:
                    pe.wait_ge(s_gl, 2)
                    pe.wait_ge(s_gc, 5)
                for c in range(5):
                    w = 512 if c < 4 else NS
                    te.matmul(ps[:, c, 0:w], rowsel[:, g, :], biasS[:, 512 * c:512 * c + w], start=True, stop=False,
                              skip_group_check=True)
                keys(16 * g)
                for j in range(16):
                    q = 16 * g + j
                    b, c = 4 * g + j // 4, j % 4
                    if j < 15:
                        keys(q + 1)
                    r0 = 32 * (j // 4)
                    pe.wait_ge(s_kca, q + 1)
                    pe.wait_ge(s_kcd, q + 1)
                    for kv in range(NKV):
                        ins = te.matmul(ps[r0:r0 + 32, c, :], qpad[:, b, kv, :], kpT[:, q % 2, kv, :],
                                        start=False, stop=True, skip_group_check=True)
                    ins.then_inc(s_ks, 1)
                    if c == 3:
                        for kv in range(NKV):
                            ins = te.matmul(ps[r0:r0 + 32, 4, 0:NS], qpad[:, b, kv, :], kT[:, kv, SEQ:NT],
                                            start=False, stop=True, skip_group_check=True)
                        if j == 15:
                            ins.then_inc(s_gb, 1)
                pe.wait_ge(s_gn, g + 1)
                for c in range(5):
                    if c >= 2:
                        pe.wait_ge(s_gc, 5 * g + c - 1)
                    if c < 4:
                        for k in range(4):
                            ins = te.transpose(ps[:, 5 + c % 2, P * k:P * k + P],
                                               pS[:, P * (4 * c + k):P * (4 * c + k) + P], ident[:, :])
                    else:
                        ins = te.transpose(ps[0:NS, 5, 0:P], pS[:, PAST:NSK], ident[:, :])
                    ins.then_inc(s_gt, 1)
                pe.wait_ge(s_gc, 5 * g + 5)
                for j in range(16):
                    n = 32 * g + 16 + j
                    r0 = 32 * (j // 4)
                    pe.wait_ge(s_pg[n % SLOTS], 16 * SPP * (n // SLOTS + 1))
                    pe.wait_ge(s_pgp[n % SLOTS], 16 * (4 - SPP) * (n // SLOTS + 1))
                    for k in range(4):
                        ins = te.matmul(ps[r0:r0 + 32, 7, 0:256], pST[:, 4 * (j % 4) + k, r0:r0 + 32],
                                        page_slot(n)[:, k, :], start=(j % 4 == 0 and k == 0), stop=False,
                                        skip_group_check=True)
                    if j % 4 == 3:
                        ins = te.matmul(ps[r0:r0 + 32, 7, 0:256], pST[0:NS, 16, r0:r0 + 32], vN[0:NS, 4, :],
                                        start=False, stop=True, skip_group_check=True)
                    ins.then_inc(s_chunk, 1)
                pe.wait_ge(s_os, g + 1)
                for kv in range(NKV):
                    ins = te.transpose(ps[:, (4, 7)[kv], 0:P], oS[:, P * kv:P * kv + P], ident[:, :])
                ins.then_inc(s_ot, 1)

            pe.wait_ge(s_gl, 4)
            pe.wait_ge(s_mix, CT)
            with pe.Fori(0, 8) as i:
                pair(P_OUT + i)
            pe.wait_ge(s_sqs, KT + 1)
            for half in range(2):
                ins = te.matmul(ps[:, 4 + half, 0:HALF], ones[:, :], sqa[:, HALF * half:HALF * half + HALF],
                                start=True, stop=True)
            ins.then_inc(s_r2, 1)
            def ffn_pe(c, first):
                p0 = P_FFN + P_CH * c
                if first:
                    tile(p0, 0, as_ready=s_n2)
                    tile(p0, 1)
                with pe.Fori(1 if first else 0, CJ) as j:
                    pair(p0 + j)
                with pe.Fori(0, 8) as i:
                    for s in range(2):
                        pe.wait_ge(s_ev, 2 * (p0 + CJ + i) + s)
                        for hf in range(2):
                            pe.wait_ge(s_hid, CJ * c + (DK[0] if hf == 0 else CJ))
                            unit(Unit(p0 + CJ + i, 2 * s + hf), s, hf, k=DK[hf], k0=DK[0] * hf, xh=hidh, xl=hidl)

            ffn_pe(0, True)
            with pe.Fori(1, CH) as c:
                ffn_pe(c, False)

            pe.wait_ge(s_ev, M_ALL)
            for i in range(5):
                if i >= 2:
                    pe.wait_ge(s_yd, i - 1)
                for kb in range(4):
                    for k in range(4):
                        ins = te.transpose(ps[0:tok[i], 4 * (i % 2) + kb, P * k:P * k + P],
                                           h[:, 4 * kb + k, P * i:P * i + tok[i]], ident[:, :])
                    ins.then_inc(s_yt, 1)


_INS = ['x_prompt', 'x_sample', 'cache_k', 'cache_v', 'cache_idx_k', 'state_conv', 'page_table', 'norm_attn', 'w_in',
        'conv_dw', 'conv_dw_bias', 'conv_ln_g', 'conv_ln_b', 'w_out', 'norm_ffn', 'w_gate', 'w_up', 'w_down',
        'norm_final']
_OUTS = [('y_prompt', (1, SEQ, D)), ('y_sample', (B, T, D)), ('k_prompt', (1, 1, SEQ, NKV, HD)),
         ('v_prompt', (1, 1, SEQ, NKV, HD)), ('idx_k_prompt', (1, 1, SEQ, ID)), ('conv_prompt', (1, 1, CK - 1, CW_)),
         ('k_sample', (1, B, T, NKV, HD)), ('v_sample', (1, B, T, NKV, HD)), ('idx_k_sample', (1, B, T, ID)),
         ('conv_sample', (1, B, CK - 1, CW_))]


def constants():
    f32 = np.float32
    pos = np.concatenate([np.arange(SEQ), np.tile(PAST + np.arange(T), B)]).astype(f32)
    rope = np.zeros((P, 4, NT), f32)
    for n, width in ((0, HD), (2, ID)):
        half = width // 2
        expo = (-(np.arange(half, dtype=f32) / f32(half))).astype(np.float64)
        freq = (np.float64(10000.0) ** expo).astype(f32)
        d = np.arange(P) % width
        ang = (pos[None, :] * freq[d % half][:, None]).astype(f32).astype(np.float64)
        rope[:, n] = np.cos(ang)
        rope[:, n + 1] = np.where(d[:, None] < half, -np.sin(ang), np.sin(ang))
    tokens = np.arange(NS)
    row = np.arange(P)
    hsel = (np.arange(IH)[:, None] == row[None, :] // T % IH).astype(f32)
    tsel = (row[:, None] % T == tokens[None, :] % T).astype(f32)
    own = (tokens[:, None] // T == tokens[None, :] // T) & (tokens[None, :] <= tokens[:, None])
    tail = np.where(own, 0.0, INVALID).astype(f32)
    rowsel = np.zeros((NS, 2, P), f32)
    for g in range(2):
        rowsel[T * (4 * g + row // 32) + row % T, g, row] = 1.0
    caus = np.where(row[None, :] <= row[:, None], 0.0, MASKED).astype(f32)
    return {'c_ident': np.eye(P, dtype=f32), 'c_rope': rope, 'c_hsel': hsel, 'c_tsel': tsel, 'c_tail': tail,
            'c_rowsel': rowsel, 'c_caus': caus}


def kernel(**inputs):
    import concourse.bacc as _bacc
    from concourse.bass_utils import run_bass_kernel_spmd as _run

    nc = _bacc.Bacc("TRN2", target_bir_lowering=False, num_devices=1)
    arrays, a, o = {}, {}, {}
    for name, v in [(n, np.ascontiguousarray(inputs[n])) for n in _INS] + list(constants().items()):
        arrays[f"in_{name}"] = v
        a[name] = nc.dram_tensor(f"in_{name}", v.shape, mybir.dt.from_np(v.dtype), kind="ExternalInput").ap()
    for name, shape in _OUTS:
        o[name] = nc.dram_tensor(f"out_{name}", shape, F32, kind="ExternalOutput").ap()
    a['xT_dram'] = nc.dram_tensor("xT_dram", (D, NT), F32, kind="Internal").ap()
    build(nc, a, o)
    r = _run(nc, [arrays], core_ids=[0])
    return tuple(r.results[0][f"out_{name}"] for name, _ in _OUTS)
```
